# Optimizing a Trainium2 kernel written in Bass

```python
import math
import jax, jax.numpy as jnp
from jax import lax
import numpy as np

D_MODEL = 1024
BATCH = 1
SEQ = 128
DEPTH = 2
DEC_BATCH = 1
DEC_SEQ = 256
PAST_LEN = 128

GRID_W = 64
ROPE_BASE = 10000.0
NORM_EPS = 1e-6
N_EVEN = (DEPTH + 1) // 2
N_ODD = DEPTH // 2
D_HALF = D_MODEL // 2
A_HEAD = 64
A_HEADS = D_HALF // A_HEAD
A_DECAY_LORA = 64
A_ICLR_LORA = 64
A_GATE_LORA = 128
GN_EPS = 64e-5
CONV_W = 3
C_HEADS = 8
C_HD = D_MODEL // C_HEADS // 2
Q_BLOCK = 128
P_HEADS = 8
P_NKEYS = 128
P_EXPERTS = P_NKEYS * P_NKEYS
P_QDIM = 256
P_TOPK = 16
P_BLOCK = 128
EVEN_SPLITS = [D_HALF, D_HALF, D_HALF, A_DECAY_LORA, A_ICLR_LORA, A_GATE_LORA, D_HALF, D_HALF, D_HALF]
EVEN_IN = 3 * D_HALF + A_DECAY_LORA + A_ICLR_LORA + A_GATE_LORA + 3 * D_HALF
ODD_IN = 3 * D_MODEL

kernel_name = "hybrid_rwkv7_shortconv_diffattn_peer_dit_step"

def rmsnorm(x, g):
    xf = x.astype(jnp.float32)
    y = xf * lax.rsqrt(jnp.mean(xf * xf, axis=-1, keepdims=True) + NORM_EPS)
    return y.astype(x.dtype) * g

def adaln(cond, w, b):
    m = jax.nn.silu(cond) @ w + b
    return jnp.split(m[:, None, :], 6, axis=-1)

def axial_rope(n_tok, dim, dtype):
    rows = n_tok // GRID_W
    row = jnp.repeat(jnp.arange(rows, dtype=jnp.float32), GRID_W)
    col = jnp.tile(jnp.arange(GRID_W, dtype=jnp.float32), rows)
    nf = dim // 4
    inv = ROPE_BASE ** (-jnp.arange(nf, dtype=jnp.float32) / nf)
    ar = row[:, None] * inv[None, :]
    ac = col[:, None] * inv[None, :]
    ang = jnp.concatenate([ar, ar, ac, ac], axis=-1)
    return jnp.cos(ang).astype(dtype), jnp.sin(ang).astype(dtype)

def apply_rope(x, cos, sin):
    h = x.shape[-1] // 2
    q = h // 2
    xr = jnp.concatenate([-x[..., q:h], x[..., :q], -x[..., h + q:], x[..., h:h + q]], axis=-1)
    return x * cos[None, :, None, None, :] + xr * sin[None, :, None, None, :]

def wkv_scan(s0, r, w, k, v, kk, a, reverse):
    def step(S, inp):
        r_t, w_t, k_t, v_t, kk_t, a_t = inp
        sa = jnp.einsum('bhvk,bhk->bhv', S, -kk_t)
        S = S * w_t[:, :, None, :] + sa[..., None] * (kk_t * a_t)[:, :, None, :] + v_t[..., None] * k_t[:, :, None, :]
        return S, jnp.einsum('bhvk,bhk->bhv', S, r_t)
    xs = tuple(jnp.moveaxis(z, 1, 0) for z in (r, w, k, v, kk, a))
    s_fin, ys = lax.scan(step, s0.astype(jnp.float32), xs, reverse=reverse)
    return s_fin, jnp.moveaxis(ys, 0, 1)

def rwkv7_bidir(r, k, v, wd, ad, gd, s0, w0, w_up, a0, a_up, g_up, k_k, k_a, r_k, ln_g, ln_b):
    B, T, _ = r.shape
    f32 = jnp.float32

    def heads(z):
        return z.astype(f32).reshape(B, T, A_HEADS, A_HEAD)

    kk = heads(k * k_k)
    kk = kk / jnp.maximum(jnp.sqrt(jnp.sum(kk * kk, axis=-1, keepdims=True)), 1e-12)
    rh, vh = heads(r), heads(v)
    tw = jnp.tanh(wd)
    outs, bons, finals = [], [], []
    for d in range(2):
        w_pre = (w0[d] + tw @ w_up[d]).astype(f32)
        decay = heads(jnp.exp(-jnp.exp(-jax.nn.softplus(-w_pre) - 0.5)))
        a = jax.nn.sigmoid(a0[d] + ad @ a_up[d])
        kd = heads(k * (1 + (a - 1) * k_a))
        s_fin, o = wkv_scan(s0[:, d], rh, decay, kd, vh, kk, heads(a), d == 1)
        outs.append(o)
        finals.append(s_fin)
        bons.append(jnp.sum(rh * kd * r_k.astype(f32), axis=-1, keepdims=True) * vh)
    o = outs[0] + outs[1]
    mu = jnp.mean(o, axis=-1, keepdims=True)
    var = jnp.mean(jnp.square(o - mu), axis=-1, keepdims=True)
    o = ((o - mu) * lax.rsqrt(var + GN_EPS)).reshape(B, T, D_HALF) * ln_g + ln_b
    o = o + (bons[0] + bons[1]).reshape(B, T, D_HALF)
    g = jax.nn.sigmoid(gd) @ g_up
    return (o * g).astype(r.dtype), jnp.stack(finals, axis=1)

def short_conv(bg, cg, hc, conv_w):
    z = cg * hc
    T = z.shape[1]
    zp = jnp.pad(z, ((0, 0), (1, 1), (0, 0)))
    y = zp[:, 0:T] * conv_w[0] + zp[:, 1:T + 1] * conv_w[1] + zp[:, 2:T + 2] * conv_w[2]
    return bg * y

def even_mixer(h, s0, w_in, w0, w_up, a0, a_up, g_up, k_k, k_a, r_k, ln_g, ln_b, conv_w, w_out):
    offs = np.cumsum(EVEN_SPLITS[:-1]).tolist()
    r, k, v, wd, ad, gd, bg, cg, hc = jnp.split(h @ w_in, offs, axis=-1)
    y_a, s_fin = rwkv7_bidir(r, k, v, wd, ad, gd, s0, w0, w_up, a0, a_up, g_up, k_k, k_a, r_k, ln_g, ln_b)
    y_b = short_conv(bg, cg, hc, conv_w)
    return jnp.concatenate([y_a, y_b], axis=-1) @ w_out, s_fin

def odd_qkv(h, w_in):
    B, T, _ = h.shape
    q, k, v = jnp.split(h @ w_in, 3, axis=-1)
    return (q.reshape(B, T, C_HEADS, 2, C_HD), k.reshape(B, T, C_HEADS, 2, C_HD),
            v.reshape(B, T, C_HEADS, 2 * C_HD))

def diff_lambda(lp, lam_init):
    lp = lp.astype(jnp.float32)
    return jnp.exp(jnp.sum(lp[0] * lp[1])) - jnp.exp(jnp.sum(lp[2] * lp[3])) + lam_init

def diff_attention(q, k, v, lam, lam_init, subln, w_out):
    B, Tq = q.shape[0], q.shape[1]
    nb = Tq // Q_BLOCK
    qb = jnp.moveaxis(q.reshape(B, nb, Q_BLOCK, C_HEADS, 2, C_HD), 1, 0)
    scale = C_HD ** -0.5

    def blk(qi):
        s = jnp.einsum('bqhjd,bkhjd->bhjqk', qi, k).astype(jnp.float32) * scale
        p = jax.nn.softmax(s, axis=-1)
        attn = p[:, :, 0] - lam * p[:, :, 1]
        return jnp.einsum('bhqk,bkhe->bqhe', attn.astype(v.dtype), v)

    o = jnp.moveaxis(lax.map(blk, qb), 0, 1).reshape(B, Tq, C_HEADS, 2 * C_HD)
    o = rmsnorm(o, subln) * (1.0 - lam_init)
    return o.reshape(B, Tq, D_MODEL) @ w_out

def peer(h, w_q, sub_keys, u_tab, v_tab):
    B, T, D = h.shape
    n = P_BLOCK
    xb = h.reshape(B * T // n, n, D)

    def block(x):
        q = (x @ w_q).reshape(n, P_HEADS, 2, P_QDIM // 2)
        s = jnp.einsum('nhjd,hjkd->nhjk', q, sub_keys).astype(jnp.float32)
        sv, si = lax.top_k(s, P_TOPK)
        cand = (sv[:, :, 0, :, None] + sv[:, :, 1, None, :]).reshape(n, P_HEADS, P_TOPK * P_TOPK)
        cidx = (si[:, :, 0, :, None] * P_NKEYS + si[:, :, 1, None, :]).reshape(n, P_HEADS, P_TOPK * P_TOPK)
        tv, ti = lax.top_k(cand, P_TOPK)
        eidx = jnp.take_along_axis(cidx, ti, axis=-1)
        gate = jax.nn.softmax(tv, axis=-1).astype(x.dtype)
        u = u_tab[eidx]
        act = jax.nn.gelu(jnp.einsum('nhkd,nd->nhk', u, x), approximate=False)
        return jnp.einsum('nhk,nhkd->nd', gate * act, v_tab[eidx])

    return lax.map(block, xb).reshape(B, T, D)

def setup_inputs(seed: int = 0) -> dict:
    key = jax.random.key(seed)
    ks = iter(jax.random.split(key, 40))

    def nrm(shape, s):
        return jax.random.normal(next(ks), shape, jnp.float32) * s

    D = D_MODEL
    return {
        'x_prompt': nrm((BATCH, SEQ, D), 1.0),
        'x_sample': nrm((DEC_BATCH, DEC_SEQ, D), 1.0),
        'c': nrm((DEC_BATCH, D), 1.0),
        'state_rwkv': nrm((DEC_BATCH, N_EVEN, 2, A_HEADS, A_HEAD, A_HEAD), 0.1),
        'cache_k': nrm((DEC_BATCH, N_ODD, PAST_LEN, C_HEADS, 2, C_HD), 1.0),
        'cache_v': nrm((DEC_BATCH, N_ODD, PAST_LEN, C_HEADS, 2 * C_HD), 1.0),
        'c_ctx': nrm((D,), 1.0),
        'w_ada': nrm((DEPTH, D, 6 * D), 0.3 * D ** -0.5),
        'b_ada': nrm((DEPTH, 6 * D), 0.02),
        'norm_mix': 1.0 + nrm((DEPTH, D), 0.05),
        'norm_ffn': 1.0 + nrm((DEPTH, D), 0.05),
        'w_in_even': nrm((N_EVEN, D, EVEN_IN), D ** -0.5),
        'rwkv_w0': nrm((N_EVEN, 2, D_HALF), 0.5),
        'rwkv_w_up': nrm((N_EVEN, 2, A_DECAY_LORA, D_HALF), 0.1 * A_DECAY_LORA ** -0.5),
        'rwkv_a0': nrm((N_EVEN, 2, D_HALF), 0.5),
        'rwkv_a_up': nrm((N_EVEN, 2, A_ICLR_LORA, D_HALF), 0.1 * A_ICLR_LORA ** -0.5),
        'rwkv_g_up': nrm((N_EVEN, A_GATE_LORA, D_HALF), A_GATE_LORA ** -0.5),
        'rwkv_k_k': 0.85 + nrm((N_EVEN, D_HALF), 0.05),
        'rwkv_k_a': 1.0 + nrm((N_EVEN, D_HALF), 0.05),
        'rwkv_r_k': nrm((N_EVEN, A_HEADS, A_HEAD), 0.1),
        'rwkv_ln_g': 1.0 + nrm((N_EVEN, D_HALF), 0.05),
        'rwkv_ln_b': nrm((N_EVEN, D_HALF), 0.02),
        'conv_w': nrm((N_EVEN, CONV_W, D_HALF), CONV_W ** -0.5),
        'w_out_even': nrm((N_EVEN, D, D), D ** -0.5),
        'w_in_odd': nrm((N_ODD, D, ODD_IN), D ** -0.5),
        'diff_lam': nrm((N_ODD, 4, C_HD), 0.1),
        'diff_subln': 1.0 + nrm((N_ODD, 2 * C_HD), 0.05),
        'w_out_odd': nrm((N_ODD, D, D), D ** -0.5),
        'peer_w_q': nrm((DEPTH, D, P_HEADS * P_QDIM), D ** -0.5),
        'peer_sub_keys': nrm((DEPTH, P_HEADS, 2, P_NKEYS, P_QDIM // 2), (P_QDIM // 2) ** -0.5),
        'peer_u': nrm((DEPTH, P_EXPERTS, D), D ** -0.5),
        'peer_v': nrm((DEPTH, P_EXPERTS, D), 0.5),
        'final_norm': 1.0 + nrm((D,), 0.05),
    }

def reference(x_prompt, x_sample, c, state_rwkv, cache_k, cache_v, c_ctx, w_ada, b_ada, norm_mix, norm_ffn,
              w_in_even, rwkv_w0, rwkv_w_up, rwkv_a0, rwkv_a_up, rwkv_g_up, rwkv_k_k, rwkv_k_a, rwkv_r_k,
              rwkv_ln_g, rwkv_ln_b, conv_w, w_out_even, w_in_odd, diff_lam, diff_subln, w_out_odd,
              peer_w_q, peer_sub_keys, peer_u, peer_v, final_norm):
    xp, xs = x_prompt, x_sample
    bp = xp.shape[0]
    cos, sin = axial_rope(xs.shape[1], C_HD, xs.dtype)
    s_zero = jnp.zeros((bp, 2, A_HEADS, A_HEAD, A_HEAD), jnp.float32)
    new_s, new_k, new_v = [], [], []
    for l in range(DEPTH):
        i = l // 2
        sh1p, sc1p, g1p, sh2p, sc2p, g2p = adaln(c_ctx[None, :], w_ada[l], b_ada[l])
        sh1s, sc1s, g1s, sh2s, sc2s, g2s = adaln(c, w_ada[l], b_ada[l])
        hp = rmsnorm(xp, norm_mix[l]) * (1 + sc1p) + sh1p
        hs = rmsnorm(xs, norm_mix[l]) * (1 + sc1s) + sh1s
        if l % 2 == 0:
            ev = (w_in_even[i], rwkv_w0[i], rwkv_w_up[i], rwkv_a0[i], rwkv_a_up[i], rwkv_g_up[i],
                  rwkv_k_k[i], rwkv_k_a[i], rwkv_r_k[i], rwkv_ln_g[i], rwkv_ln_b[i], conv_w[i], w_out_even[i])
            yp, sp = even_mixer(hp, s_zero, *ev)
            ys, _ = even_mixer(hs, state_rwkv[:, i], *ev)
            new_s.append(sp)
        else:
            lam_init = 0.8 - 0.6 * math.exp(-0.3 * l)
            lam = diff_lambda(diff_lam[i], lam_init)
            qp, kp, vp = odd_qkv(hp, w_in_odd[i])
            yp = diff_attention(qp, kp, vp, lam, lam_init, diff_subln[i], w_out_odd[i])
            qs, ks_, vs = odd_qkv(hs, w_in_odd[i])
            k_all = jnp.concatenate([apply_rope(ks_, cos, sin), cache_k[:, i].astype(ks_.dtype)], axis=1)
            v_all = jnp.concatenate([vs, cache_v[:, i].astype(vs.dtype)], axis=1)
            ys = diff_attention(apply_rope(qs, cos, sin), k_all, v_all, lam, lam_init, diff_subln[i], w_out_odd[i])
            new_k.append(kp)
            new_v.append(vp)
        xp = xp + g1p * yp
        xs = xs + g1s * ys
        hp = rmsnorm(xp, norm_ffn[l]) * (1 + sc2p) + sh2p
        hs = rmsnorm(xs, norm_ffn[l]) * (1 + sc2s) + sh2s
        xp = xp + g2p * peer(hp, peer_w_q[l], peer_sub_keys[l], peer_u[l], peer_v[l])
        xs = xs + g2s * peer(hs, peer_w_q[l], peer_sub_keys[l], peer_u[l], peer_v[l])
    y_prompt = rmsnorm(xp, final_norm)
    y_sample = rmsnorm(xs, final_norm)
    new_state_rwkv = jnp.stack(new_s, axis=1)
    new_cache_k = jnp.stack(new_k, axis=1)
    new_cache_v = jnp.stack(new_v, axis=1)
    return (y_prompt, y_sample, new_state_rwkv, new_cache_k, new_cache_v)


_drawn_inputs = setup_inputs


def setup_inputs(seed=0):
    import zlib

    import numpy as np

    out = dict(_drawn_inputs(seed))
    spreads = {}
    factors = {'state_rwkv': 8.0,
     'norm_ffn': 3.4,
     'rwkv_w_up': 4.893,
     'rwkv_k_k': 7.207,
     'rwkv_ln_g': 8.0,
     'rwkv_ln_b': 8.0,
     'diff_lam': 4.708,
     'diff_subln': 8.0}
    for name, (base, spread) in spreads.items():
        noise = np.random.default_rng([zlib.crc32(name.encode()), seed]).standard_normal(out[name].shape)
        drawn = base * np.exp(spread * noise) if base else spread * noise
        out[name] = __import__('jax').numpy.asarray(drawn.astype(out[name].dtype))
    for name, factor in factors.items():
        out[name] = (out[name] * factor).astype(out[name].dtype)
    return out
```

```python
import math
from contextlib import ExitStack

import concourse.bass as bass
from concourse import mybir

F32 = mybir.dt.float32
U32 = mybir.dt.uint32
ALU = mybir.AluOpType
ACT = mybir.ActivationFunctionType
AX_X = mybir.AxisListType.X

P = 128
D = 1024
DC = D // P
NT = 3
T = NT * P
COND = [0, 1, 1]
NH = 8
HD = 64
NF = 4
RING = 8
LAG = 32
NJ = 128
TOPK = 16
GBLK = 16
NBLK = T // GBLK
GJ = 8
NORM_EPS = 1e-6
GN_EPS = 64e-5
LAM_INIT = 0.8 - 0.6 * math.exp(-0.3)
N_MIX_IN = [26, 24]
LAYER_TILES = [48 + n + 8 + 16 + 2 * NJ for n in N_MIX_IN]
LEVELS = 7
N_PARAM_LOADS = 3
UNITS = [(0, 0), (1, 0), (0, 1), (1, 2), (0, 2), (1, 1)]

N_FILLS = len(UNITS) * (3 + 10 + 6 * (LEVELS - 2) + 4 + 4) + 4

FEAT = {}
_at = 0
for _name, _n in [("w0", 8), ("a0", 8), ("k_k", 4), ("k_a", 4), ("r_k", 4), ("ln_g", 4), ("ln_b", 4),
                  ("conv", 12), ("norm_mix", 16), ("norm_ffn", 16), ("b_ada", 96), ("cond", 16), ("subln", 1), ("eps", 2)]:
    FEAT[_name] = _at
    _at += _n
N_FEAT = _at
CONST = {n: i for i, n in enumerate(["ident", "ones", "head_ones", "iota", "rot", "upper", "lower", "upper_eq",
                                     "lower_eq"])}
N_CONST = len(CONST)


def stage_tiles(layer):
    at = sum(LAYER_TILES[:layer])
    out = {}
    for name, n in (("ada", 48), ("mix_in", N_MIX_IN[layer]), ("mix_out", 8), ("query", 16), ("peer", 2 * NJ)):
        out[name] = at
        at += n
    return out


def bc(ap, axis, n):
    a = ap.unsqueeze(axis)
    shape = list(a.shape)
    shape[axis] = n
    return a.broadcast_to(shape)


def build(nc, A):
    with ExitStack() as ctx:
        def sb(name, shape, dt=F32):
            return ctx.enter_context(nc.sbuf_tensor(name, shape, dt))

        def sem(name):
            return ctx.enter_context(nc.semaphore(name))

        ps = ctx.enter_context(nc.psum_tensor("ps", [P, 8, 512], F32))
        x = sb("x", [P, NT, D])
        hT = sb("hT", [P, DC, T])
        ring = sb("ring", [P, RING, D])
        const = sb("const", [P, N_CONST, P])
        feats = sb("feats", [P, N_FEAT])
        silu_c = sb("silu_c", [P, DC, 2])
        mods = sb("mods", [P, 48, 2])
        mod_scale = sb("mod_scale", [P, 2, DC, 2])
        gate_bc = sb("gate_bc", [P, 2, D])
        xn = sb("xn", [P, NT, D])
        stat = sb("stat", [P, 96])
        arena = sb("arena", [P, 32000])
        g_dram = nc.dram_tensor("g_dram", [NBLK, P, P, GBLK], F32).ap()

        ident, ones, head_ones, iota, rot = (const[:, CONST[n], :] for n in ("ident", "ones", "head_ones", "iota", "rot"))

        def cm(name):
            return const[:, CONST[name], :]

        def ft(name, i=0, n=1):
            return feats[:, FEAT[name] + i:FEAT[name] + i + n]

        def area(at, *dims):
            n = 1
            for d_ in dims:
                n *= d_
            ap = arena[:, at:at + n]
            if len(dims) == 2:
                ap = ap.rearrange("p (a b) -> p a b", a=dims[0])
            elif len(dims) == 3:
                ap = ap.rearrange("p (a b c) -> p a b c", a=dims[0], b=dims[1])
            elif len(dims) == 4:
                ap = ap.rearrange("p (a b c d) -> p a b c d", a=dims[0], b=dims[1], c=dims[2])
            return ap

        hTf = hT[:, :, :].rearrange("p c t -> p (c t)")
        proj = area(0, 26, T)
        R_, K_, V_, WA, GD, BG, CG, HC = 0, 4, 8, 12, 13, 14, 18, 22
        YT_EVEN = 10
        dirv = [area(9984 + d * 6144, 4, NF, T) for d in range(2)]
        KAP, BET, GAM, RHO = range(4)
        lam = [area(22272 + d * 1536, NF, T) for d in range(2)]
        aa = [area(22272 + 3072 + d * 1536, NF, T) for d in range(2)]
        mat = area(22272, 2, 7, 4, P)
        ATM, AKM, RBM, RGM, XM, XTM, PM = range(7)
        kk = area(28416, NF, T)
        kdsum = area(29952, NF, T)
        rows = area(29440, 3, 512)
        rhs_s = area(29440 + 1536, 512)
        sa_s = area(29440 + 2048, 512)
        zst = [hTf[:, 2560 + d * 256:2816 + d * 256].rearrange("p (f v) -> p f v", f=NF) for d in range(2)]
        oT = proj[:, K_:K_ + NF, :]
        gT = proj[:, CG:CG + NF, :]
        qs = xn[:, :, :].rearrange("p a b -> p (a b)")[:, 0:1536].rearrange("p (f t) -> p f t", f=NF)
        ql = xn[:, :, :].rearrange("p a b -> p (a b)")[:, 1536:3072].rearrange("p (f t) -> p f t", f=NF)
        lvl = gate_bc[:, :, :].rearrange("p a b -> p (a b)")[:, 0:2 * LEVELS * P].rearrange("p (d l m) -> p d l m", d=2, l=LEVELS)
        half = [stat[:, 12 * d:12 * d + 12] for d in range(2)]
        dec = [stat[:, 24 + 12 * d:36 + 12 * d] for d in range(2)]
        omka = stat[:, 48:52]
        norm_ss = stat[:, 52:67]
        norm_std = stat[:, 67:82]
        lora = hTf[:, 0:1024].rearrange("p (d n) -> p d n", d=2)
        gup = hTf[:, 1024:1536]
        scan_mask = hTf[:, 1536:1536 + T]
        sfin = hTf[:, 2048:2560].rearrange("p (d f v) -> p d f v", d=2, f=NF)
        upd = area(0, 2, 512)
        nil = stat[:, 90:91]
        s0 = xn[:, :, :].rearrange("p a b -> p (a b)")[:, 0:512].rearrange("p (d f v) -> p d f v", d=2, f=NF)

        qk = area(0, 16, T)
        vrow = area(6144, NT, D)
        ckT = area(9216, 8, P)
        cv = area(10240, D)
        orow = area(11264, NT, D)
        yT_odd = area(14336, DC, T)
        pe_ = area(17408, 2, 2, T)
        pT = area(18944, 2, NT, P)
        krow = area(19712, D)
        osq = area(20736, NT, D)
        lamv = area(23808, 256)
        ropet = area(24064, 2, 256)
        sm = area(24576, 2, 16)
        oss = area(24640, 24)
        lamc = area(24672, 4)
        ropec = area(24704, 2, 256)

        acts = area(0, LAG, T)
        qT = area(12288, 16, T)
        skT = area(18432, 16, P)
        selp = area(12288, 2, 1024)
        onehot = area(12288 + 2048, 2, 2, 4, P)
        gstage = area(12288 + 4096, 2, P, GBLK)
        gtile = area(12288, 2, NBLK, GJ * GBLK)
        sc = area(20480, NT, 16, P)
        ga = area(26624, 4, T)
        selT = area(28160, 3, P)
        SM = 29312
        sv = area(SM, 16, TOPK)
        si = area(SM + 256, 16, TOPK).bitcast(U32)
        sif = area(SM + 512, 16, TOPK)
        tv = area(SM + 768, NH, TOPK)
        ti = area(SM + 896, NH, TOPK).bitcast(U32)
        tab = area(SM + 1024, 2, 128).bitcast(U32)
        tabf = area(SM + 1280, 2, 128)
        sel3 = area(SM + 1536, 3, 128)
        gsum = area(SM + 1920, 2, 8)
        fin_g = area(20480, D)
        cand = xn[:, :, :].rearrange("p a b -> p (a b)")[:, 0:2048].rearrange("p (h c) -> p h c", h=NH)

        landed = [sem(f"weight_landed{i}") for i in range(RING)]
        multiplied = sem("multiplied")
        params_in = sem("params_in")
        x_in = sem("x_in")
        state_in = sem("state_in")
        cond_sig = sem("cond_sig")
        silu_ready = sem("silu_ready")
        mods_ready = sem("mods_ready")
        x_updated = sem("x_updated")
        std_ready = sem("std_ready")
        xn_ready = sem("xn_ready")
        xT_ready = sem("xT_ready")
        hT_by_act = sem("hT_by_act")
        hT_by_dve = sem("hT_by_dve")
        proj_taken = sem("proj_taken")
        diag_ready = sem("diag_ready")
        gate_ready = sem("gate_ready")
        gate_taken = sem("gate_taken")
        conv_done = sem("conv_done")
        lora_act = sem("lora_act")
        lora_ready = sem("lora_ready")
        lora_taken = sem("lora_taken")
        ksq_ready = sem("ksq_ready")
        knorm_ready = sem("knorm_ready")
        knorm_root = sem("knorm_root")
        q_ready = sem("q_ready")
        exp_ready = sem("exp_ready")
        rkd_ready = sem("rkd_ready")
        bonus_ready = sem("bonus_ready")
        prep_done = sem("prep_done")
        fill_ready = sem("fill_ready")
        fill_taken = sem("fill_taken")
        state_ready = sem("state_ready")
        gn_ready = sem("gn_ready")
        gn_in = sem("gn_in")
        gn_root = sem("gn_root")
        y_even_ready = sem("y_even_ready")
        rot_ready = sem("rot_ready")
        rot_taken = sem("rot_taken")
        roped = sem("roped")
        v_ready = sem("v_ready")
        v_taken = sem("v_taken")
        krow_ps = sem("krow_ps")
        krow_ready = sem("krow_ready")
        caches_in = sem("caches_in")
        lam_sums = sem("lam_sums")
        lam_exp = sem("lam_exp")
        sc_ready = sem("sc_ready")
        mx_ready = sem("mx_ready")
        pexp_ready = sem("pexp_ready")
        attn_ready = sem("attn_ready")
        pT_ready = sem("pT_ready")
        pT_taken = sem("pT_taken")
        o_ready = sem("o_ready")
        o_taken = sem("o_taken")
        on_sums = sem("on_sums")
        on_root = sem("on_root")
        on_ready = sem("on_ready")
        oT_ready = sem("oT_ready")
        y_odd_ready = sem("y_odd_ready")
        lora_in = sem("lora_in")
        keys_in = sem("keys_in")
        fin_in = sem("fin_in")
        scores_ready = sem("scores_ready")
        scores_taken = sem("scores_taken")
        gexp_in = sem("gexp_in")
        gexp_ready = sem("gexp_ready")
        sel_ready = sem("sel_ready")
        selT_ready = sem("selT_ready")
        selT_taken = sem("selT_taken")
        onehot_ready = sem("onehot_ready")
        g_ready = sem("g_ready")
        g_taken = sem("g_taken")
        g_stored = [sem(f"g_stored{i}") for i in range(2)]
        g_in = [sem(f"g_in{i}") for i in range(2)]
        gelu_done = sem("gelu_done")
        ga_ready = sem("ga_ready")
        outs_done = sem("outs_done")
        onehots_read = sem("onehots_read")
        dve_order = sem("dve_order")
        act_order = sem("act_order")

        def mix_y(layer):
            return proj[:, YT_EVEN:YT_EVEN + DC, :] if layer == 0 else yT_odd

        block = ctx.enter_context(nc.Block())

        @block.sync
        def _(sp):
            sp.dma_start(feats[:, :], A["feats"]).then_inc(params_in, 16)
            sp.dma_start(const[:, :, :], A["const"]).then_inc(params_in, 16)
            sp.dma_start(x[:, 0, :], A["x_prompt"]).then_inc(x_in, 16)
            sp.dma_start(x[:, 1:3, :], A["x_sample"].rearrange("(t p) d -> p t d", p=P)).then_inc(x_in, 16)
            sp.dma_start(lvl, A["levels"]).then_inc(params_in, 16)

            def load_tile(src, g0, k, it):
                g = g0 + k
                slot = g % RING
                if g >= RING or not isinstance(it, int):
                    sp.wait_ge(multiplied, (g - RING + 1) + it * RING)
                sp.dma_start(ring[:, slot, :], src).then_inc(landed[slot], 16)

            def load_all(src, g0, n):
                loops = n // RING
                rest = 0
                if g0 < RING:
                    for k in range(RING):
                        load_tile(src[k], g0, k, 0)
                    rest = RING
                    loops -= 1
                if loops > 0:
                    with sp.Fori(0, loops) as i:
                        for k in range(RING):
                            load_tile(src[bass.ds(i * RING + rest + k, 1)].rearrange("a p n -> (a p) n"),
                                      g0 + rest, k, i)
                for n0 in range(rest + loops * RING, n):
                    load_tile(src[n0], g0, n0, 0)

            for layer in range(2):
                at = stage_tiles(layer)
                load_all(A[f"ada{layer}"], at["ada"], 48)
                load_all(A[f"mix_in{layer}"], at["mix_in"], N_MIX_IN[layer])
                load_all(A[f"mix_out{layer}"], at["mix_out"], 8)
                load_all(A[f"query{layer}"], at["query"], 16)
                g0 = at["peer"]
                u, v = A[f"u{layer}"], A[f"v{layer}"]
                load_all(u, g0, LAG)
                g0 += LAG
                with sp.Fori(0, (NJ - LAG) // 4) as i:
                    for k in range(4):
                        load_tile(u[bass.ds(i * 4 + LAG + k, 1)].rearrange("a p n -> (a p) n"), g0, 2 * k, i)
                        load_tile(v[bass.ds(i * 4 + k, 1)].rearrange("a p n -> (a p) n"), g0, 2 * k + 1, i)
                g0 += 2 * (NJ - LAG)
                with sp.Fori(0, LAG // RING) as i:
                    for k in range(RING):
                        load_tile(v[bass.ds(i * RING + NJ - LAG + k, 1)].rearrange("a p n -> (a p) n"), g0, k, i)

        @block.tensor
        def _(pe):
            def tile_landed(g0, k, it=0):
                g = g0 + k
                pe.wait_ge(landed[g % RING], 16 * (g // RING + 1) + it * 16)
                return ring[:, g % RING, :].rearrange("p (c n) -> p c n", c=DC)

            def ada(layer):
                if layer == 0:
                    pe.wait_ge(silu_ready, 1)
                for n in range(48):
                    w = tile_landed(stage_tiles(layer)["ada"], n)
                    for c in range(DC):
                        mm = pe.matmul(ps[:, 7, 2 * n:2 * n + 2], w[:, c, :], silu_c[:, c, :],
                                       start=(c == 0), stop=(c == DC - 1))
                    mm.then_inc(multiplied, 1)

            def norm_T(n):
                if n == 0:
                    pe.wait_ge(params_in, 16 * N_PARAM_LOADS)
                for t in range(NT):
                    pe.wait_ge(xn_ready, NT * n + t + 1)
                    for hf in range(2):
                        for c in range(4):
                            mm = pe.transpose(ps[:, 2 * t + hf, c * P:(c + 1) * P],
                                              xn[:, t, (4 * hf + c) * P:(4 * hf + c + 1) * P], ident)
                        mm.then_inc(xT_ready, 1)
                pe.wait_ge(hT_by_act, NT * (n + 1))
                pe.wait_ge(hT_by_dve, NT * (n + 1))

            def project(g0, count, base):
                for n in range(count):
                    w = tile_landed(g0, n)
                    if n >= 4:
                        pe.wait_ge(proj_taken, base + n - 3)
                    for c in range(DC):
                        mm = pe.matmul(ps[:, n % 4, 0:T], w[:, c, :], hT[:, c, :], start=(c == 0), stop=(c == DC - 1))
                    mm.then_inc(multiplied, 1)

            def row_project(g0, act, first_wait=None):
                for nb in range(2):
                    for q in range(4):
                        g = g0 + nb * 4 + q
                        pe.wait_ge(landed[g % RING], 16 * (g // RING + 1))
                        w = ring[:, g % RING, :].rearrange("p (c n) -> p c n", c=2)
                        for cc in range(2):
                            c = 2 * q + cc
                            for t in range(NT):
                                mm = pe.matmul(ps[:, 3 * nb + t, :], act[:, c, t * P:(t + 1) * P], w[:, cc, :],
                                               start=(c == 0), stop=(c == DC - 1))
                        mm.then_inc(multiplied, 1)

            def gate_rows(n):
                for q in range(4):
                    pe.wait_ge(diag_ready, 4 * n + q + 1)
                    if q >= 2:
                        pe.wait_ge(gate_taken, 4 * n + q - 1)
                    pe.matmul(ps[:, 6 + q % 2, :], ones, xn[:, 0:2, :].rearrange("p a b -> p (a b)")[:, 512 * q:512 * q + 512],
                              start=True, stop=True).then_inc(gate_ready, 1)

            def rwkv_prep():
                pe.wait_ge(lora_act, 2)
                pe.wait_ge(lora_in, 48)
                for m in range(20):
                    if m >= 4:
                        pe.wait_ge(lora_taken, m - 3)
                    if m < 16:
                        d, f, wa = m // 8, m % 4, (m // 4) % 2
                        k0 = HD * wa
                        mm = pe.matmul(ps[:, m % 4, 0:T], lora[k0:k0 + HD, d, f * P:(f + 1) * P],
                                       proj[k0:k0 + HD, WA, :], start=True, stop=True)
                    else:
                        f = m % 4
                        mm = pe.matmul(ps[:, m % 4, 0:T], gup[:, f * P:(f + 1) * P], proj[:, GD, :], start=True, stop=True)
                    mm.then_inc(lora_ready, 1)
                pe.wait_ge(ksq_ready, 1)
                for f in range(NF):
                    pe.matmul(ps[:, 4 + f, 0:T], head_ones, qs[:, f, :], start=True, stop=True).then_inc(knorm_ready, 1)
                pe.wait_ge(rkd_ready, 1)
                for f in range(NF):
                    pe.matmul(ps[:, 4 + f, 0:T], head_ones, qs[:, f, :], start=True, stop=True).then_inc(bonus_ready, 1)

            def rwkv_units():
                n = [0]

                def open_bank(need=None):
                    w = max(n[0] - 5, 0 if need is None else need + 1)
                    if w > 0:
                        pe.wait_ge(fill_taken, w)
                    b = n[0] % 6
                    n[0] += 1
                    return b

                pe.wait_ge(prep_done, 1)
                for q, (d, t) in enumerate(UNITS):
                    ts = slice(t * P, (t + 1) * P)
                    dv = dirv[d]
                    for src in (dv[:, BET], dv[:, GAM], proj[:, V_:V_ + NF]):
                        b = open_bank()
                        for f in range(NF):
                            mm = pe.transpose(ps[:, b, f * P:(f + 1) * P], src[:, f, ts], ident)
                        mm.then_inc(fill_ready, 1)

                    def head(h4, hf):
                        return h4, slice(HD * hf, HD * hf + HD)

                    for l_, r_ in ((BET, KAP), (KAP, BET), (GAM, KAP), (BET, RHO), (GAM, RHO)):
                        for hf in range(2):
                            b = open_bank()
                            for h4 in range(4):
                                f, kp = head(h4, hf)
                                mm = pe.matmul(ps[:, b, h4 * P:(h4 + 1) * P], dv[kp, l_, f, ts], dv[kp, r_, f, ts],
                                               start=True, stop=True)
                            mm.then_inc(fill_ready, 1)
                    base = n[0]
                    last_x = [base - 10 + 2, base - 10 + 3]
                    for lv in range(1, LEVELS):
                        p_at = n[0]
                        for hf in range(2):
                            b = open_bank(last_x[hf])
                            for h4 in range(4):
                                mm = pe.matmul(ps[:, b, h4 * P:(h4 + 1) * P], mat[:, hf, ATM, h4, :], mat[:, hf, XM, h4, :],
                                               start=True, stop=True)
                            mm.then_inc(fill_ready, 1)
                        if lv < LEVELS - 1:
                            for hf in range(2):
                                b = open_bank(p_at + hf)
                                for h4 in range(4):
                                    mm = pe.matmul(ps[:, b, h4 * P:(h4 + 1) * P], mat[:, hf, XTM, h4, :],
                                                   mat[:, hf, PM, h4, :], start=True, stop=True)
                                mm.then_inc(fill_ready, 1)
                        xt_at = n[0]
                        for hf in range(2):
                            b = open_bank(p_at + hf)
                            for h4 in range(4):
                                mm = pe.matmul(ps[:, b, h4 * P:(h4 + 1) * P], mat[:, hf, PM, h4, :],
                                               mat[:, hf, XTM, h4, :], start=True, stop=True)
                            mm.then_inc(fill_ready, 1)
                        last_x = [xt_at, xt_at + 1]
                    if q in (2, 3):
                        pe.wait_ge(state_ready, q - 1)
                    for hf in range(2):
                        b = open_bank(last_x[1] if hf == 0 else None)
                        for h4 in range(4):
                            f, kp = head(h4, hf)
                            h = 2 * h4 + hf
                            o = ps[:, b, h4 * HD:(h4 + 1) * HD]
                            if t > 0:
                                pe.matmul(o, dv[kp, KAP, f, ts], zst[d][kp, f, :], start=True, stop=False)
                            mm = pe.matmul(o, mat[:, hf, AKM, h4, :], rows[:, 2, h * HD:(h + 1) * HD],
                                           start=(t == 0), stop=True)
                        mm.then_inc(fill_ready, 1)
                    b = open_bank(n[0] - 1)
                    for h in range(NH):
                        mm = pe.matmul(ps[:, b, h * HD:(h + 1) * HD], mat[:, h % 2, XTM, h // 2, :],
                                       rhs_s[:, h * HD:(h + 1) * HD], start=True, stop=True)
                    mm.then_inc(fill_ready, 1)
                    b = open_bank(n[0] - 1)
                    for h in range(NH):
                        f, kp = head(h // 2, h % 2)
                        o = ps[kp, b, f * P:(f + 1) * P]
                        hs = slice(h * HD, (h + 1) * HD)
                        if t > 0:
                            pe.matmul(o, zst[d][kp, f, :], dv[kp, RHO, f, ts], start=True, stop=False)
                        pe.matmul(o, rows[:, 2, hs], mat[:, h % 2, RGM, h // 2, :], start=(t == 0), stop=False)
                        mm = pe.matmul(o, sa_s[:, hs], mat[:, h % 2, RBM, h // 2, :], start=False, stop=True)
                    mm.then_inc(fill_ready, 1)
                    if q < 4:
                        b = open_bank()
                        for h in range(NH):
                            f, kp = head(h // 2, h % 2)
                            o = ps[kp, b, f * HD:(f + 1) * HD]
                            hs = slice(h * HD, (h + 1) * HD)
                            pe.matmul(o, rows[:, 0, hs], sa_s[:, hs], start=True, stop=False)
                            mm = pe.matmul(o, rows[:, 1, hs], rows[:, 2, hs], start=False, stop=True)
                        mm.then_inc(fill_ready, 1)

            def group_norm():
                pe.wait_ge(gn_in, 1)
                for f in range(NF):
                    pe.matmul(ps[:, f, 0:T], head_ones, oT[:, f, :], start=True, stop=True).then_inc(gn_ready, 1)
                pe.wait_ge(gn_in, 2)
                for f in range(NF):
                    pe.matmul(ps[:, 4 + f, 0:T], head_ones, kk[:, f, :], start=True, stop=True).then_inc(gn_ready, 1)

            def attention():
                pe.wait_ge(v_taken, 6)
                for n in range(16):
                    pe.wait_ge(proj_taken, 26 + 16 + n + 1)
                    if n >= 2:
                        pe.wait_ge(rot_taken, n - 1)
                    pe.matmul(ps[:, 4 + n % 2, 0:256], rot, qk[:, n, P:T], start=True, stop=True).then_inc(rot_ready, 1)
                for hf in range(2):
                    for c in range(4):
                        mm = pe.transpose(ps[:, 6 + hf, c * P:(c + 1) * P], qk[:, 8 + 4 * hf + c, 0:P], ident)
                    mm.then_inc(krow_ps, 1)
                pe.wait_ge(krow_ready, 2)
                pe.wait_ge(caches_in, 64)
                pe.wait_ge(roped, 16)
                units = [(t, h) for t in range(NT) for h in range(NH)]

                def scores(n):
                    t, h = units[n]
                    if n >= 2:
                        pe.wait_ge(pexp_ready, 2 * (n - 1))
                    for j in range(2):
                        kp = slice(HD * j, HD * j + HD)
                        o = ps[:, 2 * (n % 2) + j, :]
                        ql_ = qk[kp, h, t * P:(t + 1) * P]
                        if t == 0:
                            mm = pe.matmul(o[:, 0:P], ql_, qk[kp, 8 + h, 0:P], start=True, stop=True)
                        else:
                            pe.matmul(o[:, 0:256], ql_, qk[kp, 8 + h, P:T], start=True, stop=True)
                            mm = pe.matmul(o[:, 256:T], ql_, ckT[kp, h, :], start=True, stop=True)
                        mm.then_inc(sc_ready, 1)

                def weights_T(n):
                    t, h = units[n]
                    pe.wait_ge(attn_ready, n + 1)
                    if n >= 2:
                        pe.wait_ge(pT_taken, n - 1)
                    for b in range(1 if t == 0 else NT):
                        mm = pe.transpose(ps[:, 4 + n % 2, b * P:(b + 1) * P], pe_[:, n % 2, 0, b * P:(b + 1) * P], ident)
                    mm.then_inc(pT_ready, 1)

                def values(n):
                    t, h = units[n]
                    pe.wait_ge(pT_taken, n + 1)
                    if n >= 2:
                        pe.wait_ge(o_taken, n - 1)
                    kt = [0] if t == 0 else [1, 2, 3]
                    for q, b in enumerate(kt):
                        v = cv[:, h * P:(h + 1) * P] if b == 3 else vrow[:, b, h * P:(h + 1) * P]
                        mm = pe.matmul(ps[:, 6 + n % 2, 0:P], pT[:, n % 2, q, :], v, start=(q == 0), stop=(q == len(kt) - 1))
                    mm.then_inc(o_ready, 1)

                scores(0)
                for n in range(24):
                    if n + 1 < 24:
                        scores(n + 1)
                    weights_T(n)
                    values(n)
                for t in range(NT):
                    pe.wait_ge(on_ready, t + 1)
                    for hf in range(2):
                        for c in range(4):
                            mm = pe.transpose(ps[:, 2 * t + hf, c * P:(c + 1) * P],
                                              orow[:, t, (4 * hf + c) * P:(4 * hf + c + 1) * P], ident)
                        mm.then_inc(oT_ready, 1)

            def peer(layer):
                at = stage_tiles(layer)["peer"]
                pe.wait_ge(keys_in, 16 * (layer + 1))
                pe.wait_ge(gate_taken, 8 * (layer + 1))
                for t in range(NT):
                    for b in range(4):
                        n = 12 * layer + 4 * t + b
                        pe.wait_ge(proj_taken, proj_base(layer) + 16)
                        if t > 0:
                            pe.wait_ge(scores_taken, n - 3)
                        for c in range(4):
                            hj = 4 * b + c
                            mm = pe.matmul(ps[:, b, c * P:(c + 1) * P], qT[:, hj, t * P:(t + 1) * P], skT[:, hj, :],
                                           start=True, stop=True)
                        mm.then_inc(scores_ready, 1)

                def u_tile(g0, k, it, n0, step, first=False):
                    w = tile_landed(g0[0], g0[1], it)
                    if not first:
                        pe.wait_ge(gelu_done, (n0 + k - 1) + it * step)
                    for c in range(DC):
                        mm = pe.matmul(ps[:, 6 + k % 2, 0:T], w[:, c, :], hT[:, c, :], start=(c == 0), stop=(c == DC - 1))
                    mm.then_inc(multiplied, 1)

                U0 = NJ * layer
                for t in range(NT + 1):
                    for k in range(8):
                        u_tile((at + 8 * t, k), k, 0, U0 + 8 * t, 0, first=(layer == 0 and t == 0 and k < 2))
                    if t == NT:
                        break
                    pe.wait_ge(sel_ready, NT * layer + t + 1)
                    pe.wait_ge(scores_taken, 12 * (layer + 1))
                    for w in range(3):
                        mm = pe.transpose(ps[:, 4, w * P:(w + 1) * P], sel3[:, w, :], ident)
                    mm.then_inc(selT_ready, 1)
                    G0 = 96 * layer + 32 * t

                    def gate_groups(g, first):
                        for k in range(2):
                            pe.wait_ge(onehot_ready, g + (k + 1))
                            if not first:
                                pe.wait_ge(g_taken, g + (k - 1))
                            for q in range(4):
                                mm = pe.matmul(ps[:, k, q * P:(q + 1) * P], onehot[:, k, 0, q, :], onehot[:, k, 1, q, :],
                                               start=True, stop=True)
                            mm.then_inc(g_ready, 1)

                    gate_groups(G0, G0 == 0)
                    with pe.Fori(1, 16) as i:
                        gate_groups(i * 2 + G0, False)
                pe.wait_ge(g_taken, 96 * (layer + 1))

                def v_mms(g, k, start, stop):
                    for t in range(NT):
                        for nb in range(2):
                            mm = pe.matmul(ps[:, 2 * t + nb, :], ga[:, k % 4, t * P:(t + 1) * P],
                                           ring[:, g % RING, nb * 512:(nb + 1) * 512], start=start, stop=stop,
                                           skip_group_check=True)
                    mm.then_inc(multiplied, 1)

                def v_wait(g, n, it, step):
                    pe.wait_ge(landed[g % RING], 16 * (g // RING + 1) + it * 16)
                    pe.wait_ge(ga_ready, (NJ * layer + n + 1) + it * step)

                g0 = at + LAG
                STEADY = (NJ - LAG) // 4
                for k in range(4):
                    u_tile((g0, 2 * k), k, 0, U0 + LAG, 0)
                    v_wait(g0 + 2 * k + 1, k, 0, 0)
                    v_mms(g0 + 2 * k + 1, k, k == 0, False)
                g0 += 8
                with pe.Fori(0, STEADY - 1) as i:
                    for k in range(4):
                        u_tile((g0, 2 * k), k, i, U0 + LAG + 4, 4)
                        v_wait(g0 + 2 * k + 1, 4 + k, i, 4)
                        v_mms(g0 + 2 * k + 1, k, False, False)
                g0 += 8 * (STEADY - 1)
                n0 = NJ - LAG
                with pe.Fori(0, LAG // RING - 1) as i:
                    for k in range(RING):
                        v_wait(g0 + k, n0 + k, i, RING)
                        v_mms(g0 + k, k, False, False)
                g0 += LAG - RING
                n0 = NJ - RING
                for k in range(RING):
                    v_wait(g0 + k, n0 + k, 0, 0)
                    v_mms(g0 + k, k, False, k == RING - 1)

            def proj_base(layer):
                return 26 if layer == 0 else 26 + 16 + 16

            for layer in range(2):
                at = stage_tiles(layer)
                if layer:
                    pe.wait_ge(x_updated, 12)
                ada(layer)
                norm_T(2 * layer)
                if layer == 0:
                    project(at["mix_in"], 26, 0)
                    pe.wait_ge(proj_taken, 26)
                    rwkv_prep()
                    rwkv_units()
                    group_norm()
                    pe.wait_ge(y_even_ready, 1)
                else:
                    project(at["mix_in"], 16, 42)
                    pe.wait_ge(proj_taken, 42 + 16)
                    row_project(at["mix_in"] + 16, hT)
                    attention()
                    pe.wait_ge(y_odd_ready, 6)
                gate_rows(2 * layer)
                row_project(at["mix_out"], mix_y(layer))
                norm_T(2 * layer + 1)
                project(at["query"], 16, proj_base(layer))
                gate_rows(2 * layer + 1)
                peer(layer)

        @block.scalar
        def _(act):
            order = [0]

            def chained(ins):
                order[0] += 1
                ins.then_inc(act_order, 1)
                act.wait_ge(act_order, order[0])

            def norm_stats(n):
                for t in range(NT):
                    if n == 0:
                        act.wait_ge(x_in, 32)
                    else:
                        act.wait_ge(x_updated, 6 * (n - 1) + 3 + t + 1)
                    col = NT * n + t
                    chained(act.activation(xn[:, t, :], x[:, t, :], ACT.Square, accum_out=norm_ss[:, col:col + 1]))
                    act.activation(norm_std[:, col:col + 1], norm_ss[:, col:col + 1], ACT.Sqrt, scale=1.0 / D,
                                   bias=ft("eps", 0)).then_inc(std_ready, 1)

            def norm_evac(n):
                w, layer = n % 2, n // 2
                act.wait_ge(mods_ready, layer + 1)
                if n == 1:
                    act.wait_ge(outs_done, 32)
                for t in range(NT):
                    act.wait_ge(xT_ready, 6 * n + 2 * t + 1)
                    for c in range(4):
                        ins = act.activation(hT[:, c, t * P:(t + 1) * P], ps[:, 2 * t, c * P:(c + 1) * P], ACT.Identity,
                                             bias=mods[:, 24 * w + c, COND[t]:COND[t] + 1],
                                             scale=mod_scale[:, w, c, COND[t]:COND[t] + 1])
                    ins.then_inc(hT_by_act, 1)

            def take_projection(g0, count, dst):
                for n in range(count):
                    act.wait_ge(multiplied, g0 + n + 1)
                    act.activation(dst[:, n, :], ps[:, n % 4, 0:T], ACT.Copy).then_inc(proj_taken, 1)

            def rwkv_prep():
                act.wait_ge(proj_taken, 26)
                act.activation(proj[0:HD, WA, :], proj[0:HD, WA, :], ACT.Tanh).then_inc(lora_act, 1)
                act.activation(proj[:, GD, :], proj[:, GD, :], ACT.Sigmoid).then_inc(lora_act, 1)
                for m in range(20):
                    d, f, wa = m // 8, m % 4, (m // 4) % 2
                    act.wait_ge(lora_ready, m + 1)
                    if m == 16:
                        act.wait_ge(conv_done, 1)
                    if m < 16:
                        act.activation([lam, aa][wa][d][:, f, :], ps[:, m % 4, 0:T], ACT.Sigmoid,
                                       bias=ft(["w0", "a0"][wa], 4 * d + f)).then_inc(lora_taken, 1)
                    else:
                        act.activation(gT[:, f, :], ps[:, m % 4, 0:T], ACT.Copy).then_inc(lora_taken, 1)
                for f in range(NF):
                    act.wait_ge(knorm_ready, f + 1)
                    act.activation(ql[:, f, :], ps[:, 4 + f, 0:T], ACT.Sqrt).then_inc(knorm_root, 1)
                for d in range(2):
                    act.wait_ge(q_ready, d + 1)
                    dv = dirv[d]
                    for dst, src, sg in (((RHO, qs, -1.0), (KAP, ql, -1.0), (GAM, qs, 1.0)) if d == 0 else
                                         ((RHO, ql, 1.0), (KAP, qs, 1.0), (GAM, ql, -1.0))):
                        act.activation(dv[:, dst], src, ACT.Exp, scale=sg).then_inc(exp_ready, 1)
                    act.activation(dec[d], half[d], ACT.Exp, scale=-1.0).then_inc(exp_ready, 1)

            def group_norm():
                for f in range(NF):
                    act.wait_ge(gn_ready, NF + f + 1)
                    act.activation(qs[:, f, :], ps[:, 4 + f, 0:T], ACT.Sqrt, scale=1.0 / HD, bias=ft("eps", 1)).then_inc(gn_root, 1)

            def attention():
                for n in range(6):
                    act.wait_ge(multiplied, stage_tiles(1)["mix_in"] + 16 + 4 * (n // 3) + 4)
                    act.activation(vrow[:, n % 3, 512 * (n // 3):512 * (n // 3) + 512], ps[:, n, :], ACT.Copy).then_inc(v_taken, 1)
                for hf in range(2):
                    act.wait_ge(krow_ps, hf + 1)
                    act.activation(krow[:, hf * 512:(hf + 1) * 512], ps[:, 6 + hf, :], ACT.Copy).then_inc(krow_ready, 1)
                act.wait_ge(lam_sums, 2)
                act.activation(lamc[:, 2:4], lamc[:, 0:2], ACT.Exp).then_inc(lam_exp, 1)
                scale = HD ** -0.5

                def exps(n):
                    nk = P if n < NH else T
                    act.wait_ge(mx_ready, n + 1)
                    for j in range(2):
                        act.activation(pe_[:, n % 2, j, 0:nk], ps[:, 2 * (n % 2) + j, 0:nk], ACT.Exp,
                                       bias=sm[:, n % 2, j:j + 1], scale=scale,
                                       accum_out=sm[:, n % 2, 2 + j:3 + j]).then_inc(pexp_ready, 1)

                exps(0)
                for n in range(24):
                    if n + 1 < 24:
                        exps(n + 1)
                    act.wait_ge(pT_ready, n + 1)
                    if n >= 2:
                        act.wait_ge(o_ready, n - 1)
                    nb = 1 if n < NH else NT
                    act.activation(pT[:, n % 2, 0:nb, :], ps[:, 4 + n % 2, 0:nb * P].rearrange("p (a b) -> p a b", a=nb),
                                   ACT.Copy).then_inc(pT_taken, 1)
                act.wait_ge(on_sums, 1)
                act.activation(oss, oss, ACT.Sqrt, scale=1.0 / P, bias=ft("eps", 0)).then_inc(on_root, 1)
                for b in range(6):
                    act.wait_ge(oT_ready, b + 1)
                    for c in range(4):
                        ins = act.activation(yT_odd[:, 4 * (b % 2) + c, (b // 2) * P:(b // 2 + 1) * P],
                                             ps[:, b, c * P:(c + 1) * P], ACT.Copy, scale=lamc[:, 3:4])
                    ins.then_inc(y_odd_ready, 1)

            def peer(layer):
                at = stage_tiles(layer)["peer"]
                for t in range(NT):
                    for b in range(4):
                        act.wait_ge(scores_ready, 12 * layer + 4 * t + b + 1)
                        act.activation(sc[:, t, 4 * b:4 * b + 4, :], ps[:, b, :].rearrange("p (a b) -> p a b", a=4),
                                       ACT.Copy).then_inc(scores_taken, 1)

                def store_block(b, blk):
                    act.dma_start(g_dram[bass.ds(blk, 1)].rearrange("a i j t -> (a i) (j t)"),
                                  gstage[:, b].rearrange("p j t -> p (j t)")).then_inc(g_stored[b], 16)

                def load_g(m, b):
                    act.dma_start(gtile[:, b], g_dram[:, :, bass.ds(m * GJ, GJ), :].rearrange("b i j t -> i b (j t)"))\
                       .then_inc(g_in[b], 16)

                for t in range(NT + 1):
                    for k in range(8):
                        act.wait_ge(multiplied, at + 8 * t + k + 1)
                        act.activation(acts[:, 8 * t + k, :], ps[:, 6 + k % 2, 0:T], ACT.Gelu).then_inc(gelu_done, 1)
                    if t == NT:
                        break
                    act.wait_ge(gexp_in, NT * layer + t + 1)
                    act.activation(tv, tv, ACT.Exp).then_inc(gexp_ready, 1)
                    G0 = 96 * layer + 32 * t
                    S0 = 12 * layer + 4 * t

                    def blocks(i, first):
                        for b in range(2):
                            if not first:
                                act.wait_ge(g_stored[b], i * 16 + 16 * S0)
                            for q in range(4):
                                k = 4 * b + q
                                act.wait_ge(g_ready, (G0 + k + 1) + i * 8)
                                act.activation(gstage[:, b, :, 4 * q:4 * q + 4].rearrange("p j t -> p t j"),
                                               ps[:, k % 2, :].rearrange("p (t j) -> p t j", t=4), ACT.Copy)\
                                   .then_inc(g_taken, 1)
                            act.wait_ge(g_taken, (G0 + 4 * b + 4) + i * 8)
                            store_block(b, i * 2 + (8 * t + b))

                    blocks(0, S0 == 0)
                    with act.Fori(1, 4) as i:
                        blocks(i, False)
                for b in range(2):
                    act.wait_ge(g_stored[b], 16 * 12 * (layer + 1))
                act.wait_ge(onehots_read, layer + 1)
                load_g(0, 0)
                load_g(1, 1)
                with act.Fori(0, (NJ - LAG) // LAG) as r:
                    with act.Fori(0, 2) as i2:
                        for b in range(2):
                            for k in range(8):
                                j0 = 8 * b + k
                                act.wait_ge(ga_ready, (NJ * layer + j0 + 1) + r * LAG + i2 * 16)
                                act.wait_ge(multiplied, (at + LAG + 2 * j0 + 1) + r * (2 * LAG) + i2 * 32)
                                act.activation(acts[:, bass.ds(i2 * 16 + j0, 1), :].rearrange("p a t -> p (a t)"),
                                               ps[:, 6 + k % 2, 0:T], ACT.Gelu).then_inc(gelu_done, 1)
                            load_g(r * 4 + i2 * 2 + (b + 2), b)
                for b in range(2):
                    act.wait_ge(ga_ready, NJ * layer + (NJ - LAG) + 8 * (b + 1))
                    load_g(14 + b, b)

            act.wait_ge(params_in, 16 * N_PARAM_LOADS)
            act.activation(silu_c[:, :, :], ft("cond", 0, 16).rearrange("p (c k) -> p c k", k=2), ACT.Sigmoid).then_inc(cond_sig, 1)
            for layer in range(2):
                at = stage_tiles(layer)
                norm_stats(2 * layer)
                norm_evac(2 * layer)
                if layer == 0:
                    take_projection(at["mix_in"], 26, proj)
                    rwkv_prep()
                    group_norm()
                else:
                    take_projection(at["mix_in"], 16, qk)
                    attention()
                norm_stats(2 * layer + 1)
                norm_evac(2 * layer + 1)
                take_projection(at["query"], 16, qT)
                peer(layer)
            norm_stats(4)

        @block.vector
        def _(dve):
            order = [0]

            def chained(ins):
                order[0] += 1
                ins.then_inc(dve_order, 1)
                dve.wait_ge(dve_order, order[0])

            def tt(out, a, b, op):
                return dve.tensor_tensor(out, a, b, op)

            def modulation(layer):
                dve.wait_ge(multiplied, stage_tiles(layer)["ada"] + 48)
                if layer:
                    dve.wait_ge(x_updated, 12)
                ba = ft("b_ada", 48 * layer, 48)
                chained(tt(mods[:, :, :], ps[:, 7, 0:96].rearrange("p (n k) -> p n k", k=2), bc(ba, 2, 2), ALU.add))
                for w in range(2):
                    nw = ft("norm_mix" if w == 0 else "norm_ffn", 8 * layer, 8)
                    ins = dve.scalar_tensor_tensor(mod_scale[:, w], mods[:, 24 * w + 8:24 * w + 16, :], 1.0, bc(nw, 2, 2),
                                                   ALU.add, ALU.mult)
                    if w == 0:
                        chained(ins)
                ins.then_inc(mods_ready, 1)

            def normalise(n):
                for t in range(NT):
                    dve.wait_ge(std_ready, NT * n + t + 1)
                    col = NT * n + t
                    chained(dve.reciprocal(norm_std[:, col:col + 1], norm_std[:, col:col + 1]))
                    ins = dve.tensor_scalar(xn[:, t, :], x[:, t, :], norm_std[:, col:col + 1], None, ALU.mult)
                    if n == 4:
                        chained(ins)
                        if t == 0:
                            dve.wait_ge(fin_in, 16)
                        ins = tt(xn[:, t, :], xn[:, t, :], fin_g, ALU.mult)
                    ins.then_inc(xn_ready, 1)

            def norm_evac(n):
                w, layer = n % 2, n // 2
                dve.wait_ge(mods_ready, layer + 1)
                if n == 1:
                    dve.wait_ge(outs_done, 32)
                for t in range(NT):
                    dve.wait_ge(xT_ready, 6 * n + 2 * t + 2)
                    for c in range(4):
                        ins = dve.tensor_scalar(hT[:, 4 + c, t * P:(t + 1) * P], ps[:, 2 * t + 1, c * P:(c + 1) * P],
                                                mod_scale[:, w, 4 + c, COND[t]:COND[t] + 1],
                                                mods[:, 24 * w + 4 + c, COND[t]:COND[t] + 1], ALU.mult, ALU.add)
                    ins.then_inc(hT_by_dve, 1)

            def gate_rows(n):
                xf = xn[:, :, :].rearrange("p a b -> p (a b)")
                w, layer = n % 2, n // 2
                for q in range(4):
                    for c4 in range(4):
                        m = 4 * q + c4
                        ins = dve.tensor_scalar(xf[:, m * P:(m + 1) * P], ident,
                                                mods[:, 24 * w + 16 + m % 8, m // 8:m // 8 + 1], None, ALU.mult)
                    ins.then_inc(diag_ready, 1)
                for q in range(4):
                    dve.wait_ge(gate_ready, 4 * n + q + 1)
                    dve.tensor_copy(gate_bc[:, q // 2, 512 * (q % 2):512 * (q % 2) + 512], ps[:, 6 + q % 2, :]).then_inc(gate_taken, 1)

            def residual(n, bank, ready):
                dve.wait_ge(gate_taken, 4 * (n + 1))
                for nb in range(2):
                    dve.wait_ge(multiplied, ready[nb])
                    for t in range(NT):
                        cols = slice(512 * nb, 512 * nb + 512)
                        tmp = upd[:, (NT * nb + t) % 2, :]
                        if NT * nb + t >= 2:
                            dve.wait_ge(x_updated, 6 * n + NT * nb + t - 1)
                        chained(tt(tmp, ps[:, bank(nb, t), :], gate_bc[:, COND[t], cols], ALU.mult))
                        tt(x[:, t, cols], x[:, t, cols], tmp, ALU.add).then_inc(x_updated, 1)

            def short_conv():
                dve.wait_ge(proj_taken, 26)
                z, y = proj[:, CG:CG + NF, :], proj[:, HC:HC + NF, :]
                chained(tt(z, z, y, ALU.mult))
                for f in range(NF):
                    ins = dve.tensor_scalar(y[:, f, :], z[:, f, :], ft("conv", 4 + f), None, ALU.mult)
                chained(ins)
                for w, lo in ((0, 1), (8, 0)):
                    for f in range(NF):
                        for a, b in ((0, P), (P, T)):
                            out = y[:, f, a + 1:b] if lo else y[:, f, a:b - 1]
                            src = z[:, f, a:b - 1] if lo else z[:, f, a + 1:b]
                            ins = dve.scalar_tensor_tensor(out, src, ft("conv", w + f), out, ALU.mult, ALU.add)
                    chained(ins)
                tt(proj[:, BG:BG + NF, :], proj[:, BG:BG + NF, :], y, ALU.mult).then_inc(conv_done, 1)

            def rwkv_prep():
                for f in range(NF):
                    ins = dve.tensor_scalar(kk[:, f, :], proj[:, K_ + f, :], ft("k_k", f), None, ALU.mult)
                chained(ins)
                tt(qs, kk, kk, ALU.mult).then_inc(ksq_ready, 1)
                chained(dve.tensor_scalar(omka, ft("k_a", 0, 4), -1.0, 1.0, ALU.mult, ALU.add))
                dve.wait_ge(knorm_root, NF)
                chained(dve.tensor_scalar(ql, ql, 1e-12, None, ALU.max))
                chained(dve.reciprocal(ql, ql))
                chained(tt(kk, kk, ql, ALU.mult))
                dve.wait_ge(lora_in, 48)
                for d in range(2):
                    dv = dirv[d]
                    dve.wait_ge(lora_taken, 8 * d + 8)
                    chained(dve.tensor_scalar(lam[d], lam[d], math.exp(-0.5), None, ALU.mult))
                    for f in range(NF):
                        ins = dve.tensor_tensor_scan(qs[:, f, :], scan_mask, lam[d][:, f, :], 0.0, ALU.mult, ALU.add)
                    chained(ins)
                    q4 = qs.rearrange("p f (t m) -> p (f t) m", t=NT)
                    chained(dve.tensor_scalar(half[d], q4[:, :, P - 1], 0.5, None, ALU.mult))
                    chained(tt(q4, q4, bc(half[d], 2, P), ALU.subtract))
                    chained(tt(ql, qs, lam[d], ALU.subtract))
                    dve.tensor_copy(nil, half[d][:, 0:1]).then_inc(q_ready, 1)
                    for f in range(NF):
                        ins = dve.tensor_scalar(lam[d][:, f, :], aa[d][:, f, :], ft("k_a", f), omka[:, f:f + 1], ALU.mult, ALU.add)
                    chained(ins)
                    chained(tt(lam[d], lam[d], proj[:, K_:K_ + NF, :], ALU.mult))
                    if d == 0:
                        dve.tensor_copy(kdsum, lam[d])
                    else:
                        tt(kdsum, kdsum, lam[d], ALU.add)
                    chained(tt(aa[d], aa[d], kk, ALU.mult))
                    dve.wait_ge(exp_ready, 4 * d + 4)
                    chained(tt(dv[:, BET], aa[d], dv[:, GAM], ALU.mult))
                    tt(dv[:, GAM], dv[:, GAM], lam[d], ALU.mult)
                    tt(dv[:, RHO], dv[:, RHO], proj[:, R_:R_ + NF, :], ALU.mult)
                    chained(tt(dv[:, KAP], dv[:, KAP], kk, ALU.mult))
                chained(tt(qs, kdsum, proj[:, R_:R_ + NF, :], ALU.mult))
                for f in range(NF):
                    ins = dve.tensor_scalar(qs[:, f, :], qs[:, f, :], ft("r_k", f), None, ALU.mult)
                ins.then_inc(rkd_ready, 1)
                for f in range(NF):
                    dve.wait_ge(bonus_ready, f + 1)
                    ins = tt(proj[:, R_ + f, :], ps[:, 4 + f, 0:T], proj[:, V_ + f, :], ALU.mult)
                dve.wait_ge(lora_taken, 20)
                ins.then_inc(prep_done, 1)

            def rwkv_units():
                n = [0]

                def filled():
                    dve.wait_ge(fill_ready, n[0] + 1)
                    b = n[0] % 6
                    n[0] += 1
                    return ps[:, b, :]

                def four(ap):
                    return ap.rearrange("p (h m) -> p h m", h=4)

                dve.wait_ge(prep_done, 1)
                for q, (d, t) in enumerate(UNITS):
                    strict_T, strict, incl = [("upper", "lower", "upper_eq"), ("lower", "upper", "lower_eq")][d]
                    for w in range(3):
                        dve.tensor_copy(rows[:, w, :], filled()).then_inc(fill_taken, 1)
                    for hf in range(2):
                        b = four(filled())
                        chained(tt(mat[:, hf, ATM], b, bc(cm(strict_T), 1, 4), ALU.mult))
                        chained(tt(mat[:, hf, XTM], mat[:, hf, ATM], bc(lvl[:, 1 - d, 0, :], 1, 4), ALU.mult))
                        tt(mat[:, hf, XTM], bc(ident, 1, 4), mat[:, hf, XTM], ALU.subtract).then_inc(fill_taken, 1)
                    for hf in range(2):
                        b = four(filled())
                        chained(tt(mat[:, hf, XM], b, bc(lvl[:, d, 0, :], 1, 4), ALU.mult))
                        tt(mat[:, hf, XM], bc(ident, 1, 4), mat[:, hf, XM], ALU.subtract).then_inc(fill_taken, 1)
                    for which, mask in ((AKM, strict_T), (RBM, incl), (RGM, incl)):
                        for hf in range(2):
                            tt(mat[:, hf, which], four(filled()), bc(cm(mask), 1, 4), ALU.mult).then_inc(fill_taken, 1)
                    for lv in range(1, LEVELS):
                        for hf in range(2):
                            tt(mat[:, hf, PM], four(filled()), bc(lvl[:, d, lv, :], 1, 4), ALU.mult).then_inc(fill_taken, 1)
                        for which in ((XM, XTM) if lv < LEVELS - 1 else (XTM,)):
                            for hf in range(2):
                                tt(mat[:, hf, which], mat[:, hf, which], four(filled()), ALU.subtract).then_inc(fill_taken, 1)
                    for hf in range(2):
                        dve.tensor_copy(rhs_s.rearrange("p (h two v) -> p h two v", two=2, v=HD)[:, :, hf, :],
                                        filled()[:, 0:256].rearrange("p (h v) -> p h v", h=4)).then_inc(fill_taken, 1)
                    dve.tensor_scalar(sa_s, filled(), -1.0, None, ALU.mult).then_inc(fill_taken, 1)
                    ot = oT[:, :, t * P:(t + 1) * P]
                    y = four(filled())
                    if q in (0, 2, 3):
                        dve.tensor_copy(ot, y).then_inc(fill_taken, 1)
                    else:
                        tt(ot, ot, y, ALU.add).then_inc(fill_taken, 1)
                    if q < 4:
                        s = filled()[:, 0:NF * HD].rearrange("p (f v) -> p f v", f=NF)
                        g = dec[d].rearrange("p (f t) -> p f t", t=NT)
                        if q < 2:
                            dve.tensor_tensor(zst[d], s, bc(g[:, :, t], 2, HD), ALU.mult).then_inc(fill_taken, 1)
                            dve.wait_ge(fill_taken, n[0])
                            chained(dve.tensor_copy(sfin[:, d], zst[d]))
                            dve.wait_ge(state_in, 16)
                            t1 = 1 if d == 0 else 2
                            tt(zst[d], s0[:, d], bc(g[:, :, t1], 2, HD), ALU.mult).then_inc(state_ready, 1)
                        else:
                            tn = 2 if d == 0 else 1
                            chained(tt(zst[d], zst[d], s, ALU.add))
                            chained(tt(zst[d], zst[d], bc(g[:, :, t], 2, HD), ALU.mult))
                            tt(zst[d], zst[d], bc(g[:, :, tn], 2, HD), ALU.mult).then_inc(fill_taken, 1)

            def group_norm():
                dve.wait_ge(fill_taken, N_FILLS)
                dve.tensor_copy(nil, half[0][:, 0:1]).then_inc(gn_in, 1)
                for f in range(NF):
                    dve.wait_ge(gn_ready, f + 1)
                    ins = dve.scalar_tensor_tensor(oT[:, f, :], ps[:, f, 0:T], -1.0 / HD, oT[:, f, :], ALU.mult, ALU.add)
                chained(ins)
                tt(kk, oT, oT, ALU.mult).then_inc(gn_in, 1)
                dve.wait_ge(gn_root, NF)
                chained(dve.reciprocal(qs, qs))
                chained(tt(oT, oT, qs, ALU.mult))
                for f in range(NF):
                    ins = dve.tensor_scalar(oT[:, f, :], oT[:, f, :], ft("ln_g", f), ft("ln_b", f), ALU.mult, ALU.add)
                chained(ins)
                chained(tt(oT, oT, proj[:, R_:R_ + NF, :], ALU.add))
                tt(proj[:, YT_EVEN:YT_EVEN + NF, :], oT, gT, ALU.mult).then_inc(y_even_ready, 1)

            def attention():
                dve.wait_ge(caches_in, 64)
                for i in range(2):
                    a = lamv[:, 128 * i:128 * i + 64]
                    b = lamv[:, 128 * i + 64:128 * i + 128]
                    dve.tensor_tensor_reduce(osq[:, 0, 0:64], a, b, 1.0, 0.0, ALU.mult, ALU.add, lamc[:, i:i + 1]).then_inc(lam_sums, 1)
                    dve.wait_ge(lam_sums, i + 1)
                for m in range(16):
                    dve.wait_ge(rot_ready, m + 1)
                    r = ropet[:, m % 2, :]
                    xq = qk[:, m, P:T]
                    if m >= 2:
                        dve.wait_ge(roped, m - 1)
                    dve.tensor_tensor(r, ps[:, 4 + m % 2, 0:256], ropec[:, 1, :], ALU.mult).then_inc(rot_taken, 1)
                    chained(tt(xq, xq, ropec[:, 0, :], ALU.mult))
                    dve.wait_ge(rot_taken, m + 1)
                    tt(xq, xq, r, ALU.add).then_inc(roped, 1)
                dve.wait_ge(lam_exp, 1)
                chained(tt(lamc[:, 0:1], lamc[:, 3:4], lamc[:, 2:3], ALU.subtract))
                chained(dve.tensor_scalar(lamc[:, 0:1], lamc[:, 0:1], -LAM_INIT, None, ALU.add))
                chained(dve.tensor_scalar(lamc[:, 3:4], ft("subln"), 1.0 - LAM_INIT, None, ALU.mult))
                scale = HD ** -0.5

                def maxes(n):
                    nk = P if n < NH else T
                    s = sm[:, n % 2, :]
                    dve.wait_ge(sc_ready, 2 * n + 2)
                    chained(dve.tensor_reduce(s[:, 0:2], ps[:, 2 * (n % 2):2 * (n % 2) + 2, 0:nk], AX_X, ALU.max))
                    dve.tensor_scalar(s[:, 0:2], s[:, 0:2], -scale, None, ALU.mult).then_inc(mx_ready, 1)

                def take_o(n):
                    t, h = n // NH, n % NH
                    dve.wait_ge(o_ready, n + 1)
                    dve.tensor_copy(orow[:, t, h * P:(h + 1) * P], ps[:, 6 + n % 2, 0:P]).then_inc(o_taken, 1)

                maxes(0)
                for n in range(24):
                    if n + 1 < 24:
                        maxes(n + 1)
                    nk = P if n < NH else T
                    s = sm[:, n % 2, :]
                    dve.wait_ge(pexp_ready, 2 * n + 2)
                    chained(dve.reciprocal(s[:, 4:6], s[:, 2:4]))
                    chained(tt(s[:, 6:7], s[:, 5:6], lamc[:, 0:1], ALU.mult))
                    chained(dve.tensor_scalar(pe_[:, n % 2, 1, 0:nk], pe_[:, n % 2, 1, 0:nk], s[:, 6:7], None, ALU.mult))
                    dve.scalar_tensor_tensor(pe_[:, n % 2, 0, 0:nk], pe_[:, n % 2, 0, 0:nk], s[:, 4:5],
                                             pe_[:, n % 2, 1, 0:nk], ALU.mult, ALU.add).then_inc(attn_ready, 1)
                    if n >= 1:
                        take_o(n - 1)
                take_o(23)
                dve.wait_ge(o_taken, 24)
                chained(tt(osq, orow, orow, ALU.mult))
                dve.tensor_reduce(oss, osq.rearrange("p t (h e) -> p (t h) e", h=NH), AX_X, ALU.add).then_inc(on_sums, 1)
                dve.wait_ge(on_root, 1)
                chained(dve.reciprocal(oss, oss))
                for t in range(NT):
                    o3 = orow[:, t, :].rearrange("p (h e) -> p h e", h=NH)
                    tt(o3, o3, bc(oss[:, NH * t:NH * t + NH], 2, P), ALU.mult).then_inc(on_ready, 1)

            def rank(layer, t):
                s = sc[:, t]
                for r in range(2):
                    lo = slice(8 * r, 8 * r + 8)
                    for hj in range(16):
                        ins = dve.max(sv[:, hj, lo], s[:, hj, :])
                    chained(ins)
                    for hj in range(16):
                        ins = dve.max_index(si[:, hj, lo], sv[:, hj, lo], s[:, hj, :])
                    if r == 0:
                        for hj in range(16):
                            ins = dve.match_replace(s[:, hj, :], sv[:, hj, lo], s[:, hj, :], -3.0e38)
                    chained(ins)
                chained(dve.tensor_copy(sif, si))
                sv4 = sv.rearrange("p (h j) k -> p h j k", j=2)
                chained(tt(cand.rearrange("p h (a b) -> p h a b", a=TOPK), bc(sv4[:, :, 0, :], 3, TOPK),
                           bc(sv4[:, :, 1, :], 2, TOPK), ALU.add))
                for r in range(2):
                    lo = slice(8 * r, 8 * r + 8)
                    for h in range(NH):
                        ins = dve.max(tv[:, h, lo], cand[:, h, :])
                    chained(ins)
                    for h in range(NH):
                        ins = dve.max_index(ti[:, h, lo], tv[:, h, lo], cand[:, h, :])
                    if r == 0:
                        for h in range(NH):
                            ins = dve.match_replace(cand[:, h, :], tv[:, h, lo], cand[:, h, :], -3.0e38)
                    chained(ins)
                chained(dve.tensor_copy(gsum[:, 1, :], tv[:, :, 0]))
                tt(tv, tv, bc(gsum[:, 1, :], 2, TOPK), ALU.subtract).then_inc(gexp_in, 1)
                tif = ti.rearrange("p h k -> p (h k)")
                dve.tensor_scalar(tab[:, 0, :], tif, 4, None, ALU.logical_shift_right)
                chained(dve.tensor_scalar(tab[:, 1, :], tif, 15, None, ALU.bitwise_and))
                chained(dve.tensor_copy(tabf, tab))
                sif4 = sif.rearrange("p (h j) k -> p h j k", j=2)
                for w in range(2):
                    for hh in range(2):
                        eq = selp[:, 0].rearrange("p (m a) -> p m a", a=TOPK)
                        pr = selp[:, 1].rearrange("p (m a) -> p m a", a=TOPK)
                        ab = tabf[:, w, 64 * hh:64 * hh + 64]
                        chained(tt(eq, bc(ab, 2, TOPK), bc(iota[:, 0:TOPK], 1, 64), ALU.is_equal))
                        src = bc(sif4[:, 4 * hh:4 * hh + 4, w, :], 2, TOPK)
                        chained(tt(pr.rearrange("p (h k) a -> p h k a", h=4), eq.rearrange("p (h k) a -> p h k a", h=4), src, ALU.mult))
                        chained(dve.tensor_reduce(sel3[:, w, 64 * hh:64 * hh + 64], pr, AX_X, ALU.add))
                dve.wait_ge(gexp_ready, NT * layer + t + 1)
                chained(dve.tensor_reduce(gsum[:, 0, :], tv, AX_X, ALU.add))
                chained(dve.reciprocal(gsum[:, 0, :], gsum[:, 0, :]))
                tt(sel3[:, 2, :].rearrange("p (h k) -> p h k", h=NH), tv, bc(gsum[:, 0, :], 2, TOPK), ALU.mult).then_inc(sel_ready, 1)
                dve.wait_ge(selT_ready, NT * layer + t + 1)
                dve.tensor_copy(selT, ps[:, 4, 0:3 * P].rearrange("p (w t) -> p w t", w=3)).then_inc(selT_taken, 1)
                dve.wait_ge(selT_taken, NT * layer + t + 1)

            def spread(layer, t):
                G0 = 96 * layer + 32 * t

                def groups(i, first):
                    for k in range(2):
                        if not first:
                            dve.wait_ge(g_ready, i * 2 + (G0 + k - 1))
                        for q in range(4):
                            tok = i * 8 + (4 * k + q)
                            dve.tensor_scalar(onehot[:, k, 0, q, :], iota, selT[:, 0, bass.ds(tok, 1)], None, ALU.is_equal)
                            ins = dve.tensor_scalar(onehot[:, k, 1, q, :], iota, selT[:, 1, bass.ds(tok, 1)],
                                                    selT[:, 2, bass.ds(tok, 1)], ALU.is_equal, ALU.mult)
                        ins.then_inc(onehot_ready, 1)

                groups(0, G0 == 0)
                with dve.Fori(1, 16) as i:
                    groups(i, False)

            def peer(layer):
                dve.wait_ge(scores_taken, 12 * (layer + 1))
                for t in range(NT):
                    rank(layer, t)
                    spread(layer, t)
                dve.wait_ge(g_ready, 96 * (layer + 1))
                dve.tensor_copy(nil, norm_std[:, 0:1]).then_inc(onehots_read, 1)
                at = stage_tiles(layer)["peer"]

                def gated(j0, i2, off, r):
                    b, k = (j0 % 16) // 8, j0 % 8
                    if k == 0:
                        dve.wait_ge(g_in[b], 16 * (8 * layer + 1 + 2 * (j0 // 32)) + i2 * 16 + (r * 32 if r is not None else 0))
                    js = j0 % 32
                    if r is not None:
                        dve.wait_ge(gelu_done, (NJ * layer + j0 + 1) + r * LAG + i2 * 16)
                        dve.wait_ge(multiplied, off + r * (2 * LAG) + i2 * 32)
                    else:
                        dve.wait_ge(gelu_done, (NJ * layer + j0 + 1) + i2 * 16)
                        dve.wait_ge(multiplied, off + i2 * 16)
                    tt(ga[:, k % 4, :].rearrange("p (b t) -> p b t", t=GBLK),
                       acts[:, bass.ds(i2 * 16 + js, 1), :].rearrange("p a (b t) -> p (a b) t", t=GBLK),
                       gtile[:, b, :, GBLK * k:GBLK * (k + 1)], ALU.mult).then_inc(ga_ready, 1)

                with dve.Fori(0, (NJ - LAG) // LAG) as r:
                    with dve.Fori(0, 2) as i2:
                        for j0 in range(16):
                            gated(j0, i2, at + LAG + 2 * j0 - 6, r)
                with dve.Fori(0, 2) as i2:
                    for j0 in range(16):
                        gated(NJ - LAG + j0, i2, at + LAG + 2 * (NJ - LAG) + j0 - 3, None)

            dve.wait_ge(params_in, 16 * N_PARAM_LOADS)
            dve.wait_ge(cond_sig, 1)
            tt(silu_c[:, :, :], silu_c[:, :, :], ft("cond", 0, 16).rearrange("p (c k) -> p c k", k=2), ALU.mult).then_inc(silu_ready, 1)
            for layer in range(2):
                at = stage_tiles(layer)
                normalise(2 * layer)
                modulation(layer)
                norm_evac(2 * layer)
                if layer == 0:
                    short_conv()
                    rwkv_prep()
                    rwkv_units()
                    group_norm()
                else:
                    attention()
                gate_rows(2 * layer)
                mo = at["mix_out"]
                residual(2 * layer, lambda nb, t: 3 * nb + t, (mo + 4, mo + 8))
                normalise(2 * layer + 1)
                norm_evac(2 * layer + 1)
                gate_rows(2 * layer + 1)
                peer(layer)
                end = at["peer"] + 2 * NJ
                residual(2 * layer + 1, lambda nb, t: 2 * t + nb, (end, end))
            normalise(4)

        @block.gpsimd
        def _(pool):
            pool.wait_ge(multiplied, stage_tiles(0)["mix_in"] + 26)
            pool.dma_start(lora, A["lora"]).then_inc(lora_in, 16)
            pool.dma_start(gup, A["gup"]).then_inc(lora_in, 16)
            pool.dma_start(scan_mask, A["scan_mask"]).then_inc(lora_in, 16)
            pool.wait_ge(prep_done, 1)
            pool.dma_start(s0, A["state"]).then_inc(state_in, 16)
            for d in range(2):
                pool.wait_ge(state_ready, d + 1)
                pool.dma_start(A["out_state"][d], sfin[:, d]).then_inc(outs_done, 16)
            pool.wait_ge(x_updated, 6)
            pool.dma_start(skT, A["keys"][0]).then_inc(keys_in, 16)
            pool.wait_ge(x_updated, 12)
            pool.dma_start(ckT, A["cache_kT"]).then_inc(caches_in, 16)
            pool.dma_start(cv, A["cache_v"]).then_inc(caches_in, 16)
            pool.dma_start(ropec, A["rope"]).then_inc(caches_in, 16)
            pool.dma_start(lamv, A["diff_lam"].partition_broadcast(P)).then_inc(caches_in, 16)
            pool.wait_ge(krow_ready, 2)
            pool.dma_start(A["out_k"], krow).then_inc(outs_done, 16)
            pool.wait_ge(v_taken, 6)
            pool.dma_start(A["out_v"], vrow[:, 0, :]).then_inc(outs_done, 16)
            pool.wait_ge(outs_done, 64)
            pool.wait_ge(x_updated, 18)
            pool.dma_start(skT, A["keys"][1]).then_inc(keys_in, 16)
            pool.wait_ge(x_updated, 19)
            pool.dma_start(fin_g, A["final_norm"].partition_broadcast(P)).then_inc(fin_in, 16)
            pool.wait_ge(xn_ready, NT * 4 + 1)
            pool.dma_start(A["y_prompt"], xn[:, 0, :]).then_inc(outs_done, 16)
            pool.wait_ge(xn_ready, NT * 4 + 3)
            pool.dma_start(A["y_sample"].rearrange("(t p) d -> p t d", p=P), xn[:, 1:3, :]).then_inc(outs_done, 16)
            pool.wait_ge(outs_done, 96)


def kernel(**inputs):
    import numpy as np
    import concourse.bacc as bacc
    from concourse.bass_utils import run_bass_kernel_spmd

    z = {k: np.asarray(v) for k, v in inputs.items()}

    def cols(a):
        return np.asarray(a).reshape(-1, P).T

    def stationary(w):
        n = w.shape[1] // P
        return w.reshape(DC, P, n, P).transpose(2, 1, 0, 3).reshape(n, P, D)

    def moving(w):
        return w.reshape(4, 2, P, 2, 512).transpose(3, 0, 2, 1, 4).reshape(8, P, D)

    arr = {}
    cond = np.stack([z["c_ctx"], z["c"][0]])
    b_ada = z["b_ada"].reshape(2, 48, P).transpose(2, 0, 1).reshape(P, 96)
    feats = [cols(z["rwkv_w0"]), cols(z["rwkv_a0"]), cols(z["rwkv_k_k"]), cols(z["rwkv_k_a"]), cols(z["rwkv_r_k"]),
             cols(z["rwkv_ln_g"]), cols(z["rwkv_ln_b"]), cols(z["conv_w"]), cols(z["norm_mix"]), cols(z["norm_ffn"]),
             b_ada, cond.reshape(2, DC, P).transpose(2, 1, 0).reshape(P, 16), cols(z["diff_subln"]),
             np.tile(np.array([[NORM_EPS, GN_EPS]], np.float32), (P, 1))]
    arr["feats"] = np.concatenate(feats, axis=1)
    a = np.arange(P)
    up = (a[None, :] > a[:, None]).astype(np.float32)
    eye = np.eye(P, dtype=np.float32)
    rot = np.zeros((P, P), np.float32)
    q = HD // 4
    for base in (0, HD):
        for g in (0, 2 * q):
            for i in range(q):
                rot[base + g + q + i, base + g + i] = -1.0
                rot[base + g + i, base + g + q + i] = 1.0
    consts = {"ident": eye, "ones": np.ones((P, P), np.float32),
              "head_ones": (a[:, None] // HD == a[None, :] // HD).astype(np.float32),
              "iota": np.tile(a.astype(np.float32), (P, 1)), "rot": rot, "upper": up, "lower": up.T,
              "upper_eq": up + eye, "lower_eq": up.T + eye}
    arr["const"] = np.stack([consts[n] for n in CONST], axis=1)
    lev = np.zeros((P, 2, LEVELS, P), np.float32)
    for lv in range(LEVELS):
        b = 1 << lv
        off = ((a[:, None] // (2 * b) == a[None, :] // (2 * b)) & (a[:, None] // b > a[None, :] // b)).astype(np.float32)
        lev[:, 0, lv, :] = off
        lev[:, 1, lv, :] = off.T
    arr["levels"] = lev
    rowp, colp = np.repeat(np.arange(4, dtype=np.float32), 64), np.tile(np.arange(64, dtype=np.float32), 4)
    inv = (np.float32(10000.0) ** (-np.arange(16, dtype=np.float32) / np.float32(16))).astype(np.float32)
    ar, ac = rowp[:, None] * inv[None, :], colp[:, None] * inv[None, :]
    ang = np.concatenate([ar, ar, ac, ac], axis=-1)
    cs = np.stack([np.cos(ang), np.sin(ang)]).transpose(2, 0, 1)
    arr["rope"] = np.concatenate([cs, cs], axis=0).astype(np.float32)
    sm = np.ones((P, T), np.float32)
    sm[:, ::P] = 0.0
    arr["scan_mask"] = sm
    arr["lora"] = np.concatenate([z["rwkv_w_up"][0].transpose(1, 0, 2), z["rwkv_a_up"][0].transpose(1, 0, 2)], axis=0)
    arr["gup"] = z["rwkv_g_up"][0]
    arr["final_norm"] = z["final_norm"]
    arr["x_prompt"] = z["x_prompt"][0]
    arr["x_sample"] = z["x_sample"][0]
    arr["state"] = z["state_rwkv"][0, 0].reshape(2, NF, 2, HD, HD).transpose(2, 4, 0, 1, 3).reshape(P, 2, NF, HD)
    arr["cache_kT"] = z["cache_k"][0, 0].reshape(P, NH, P).transpose(2, 1, 0)
    arr["cache_v"] = z["cache_v"][0, 0].reshape(P, D)
    arr["diff_lam"] = z["diff_lam"][0].reshape(4 * HD)
    arr["keys"] = z["peer_sub_keys"].reshape(2, 16, P, P).transpose(0, 3, 1, 2)
    for layer in range(2):
        arr[f"ada{layer}"] = stationary(z["w_ada"][layer])
        arr[f"query{layer}"] = stationary(z["peer_w_q"][layer])
        arr[f"mix_out{layer}"] = moving(z["w_out_even" if layer == 0 else "w_out_odd"][0])
        arr[f"u{layer}"] = z["peer_u"][layer].reshape(P, NJ, DC, P).transpose(1, 3, 2, 0).reshape(NJ, P, D)
        arr[f"v{layer}"] = z["peer_v"][layer].reshape(P, NJ, D).transpose(1, 0, 2)
    arr["mix_in0"] = stationary(z["w_in_even"][0])
    wo = z["w_in_odd"][0]
    arr["mix_in1"] = np.concatenate([stationary(wo[:, 0:2 * D]), moving(wo[:, 2 * D:])], axis=0)
    arr = {k: np.ascontiguousarray(v) for k, v in arr.items()}

    nc = bacc.Bacc("TRN2", target_bir_lowering=False, num_devices=1)
    A = {}
    for k, v in arr.items():
        A[k] = nc.dram_tensor(f"in_{k}", v.shape, mybir.dt.from_np(v.dtype), kind="ExternalInput").ap()
    outs = {"y_prompt": (P, D), "y_sample": (2 * P, D), "out_state": (2, P, NF, HD), "out_k": (P, D), "out_v": (P, D)}
    for k, shape in outs.items():
        A[k] = nc.dram_tensor(k, shape, F32, kind="ExternalOutput").ap()
    build(nc, A)
    r = run_bass_kernel_spmd(nc, [{f"in_{k}": v for k, v in arr.items()}], core_ids=[0]).results[0]
    st = r["out_state"].reshape(2, 2, HD, NF, HD)
    st = st.transpose(0, 3, 1, 4, 2).reshape(1, 1, 2, NH, HD, HD)
    return (r["y_prompt"].reshape(1, P, D), r["y_sample"].reshape(1, 2 * P, D), np.ascontiguousarray(st),
            r["out_k"].reshape(1, 1, P, NH, 2, HD), r["out_v"].reshape(1, 1, P, NH, 2 * HD))
```

```python
import math
from contextlib import ExitStack

import concourse.bass as bass
from concourse import mybir

F32 = mybir.dt.float32
F32R = mybir.dt.float32r
U32 = mybir.dt.uint32
ALU = mybir.AluOpType
ACT = mybir.ActivationFunctionType
AX_X = mybir.AxisListType.X

P = 128
D = 1024
DC = D // P
NT = 3
T = NT * P
COND = [0, 1, 1]
NH = 8
HD = 64
NF = 4
RING = 4
UNROLL = 8
LAG = 32
NJ = 128
TOPK = 16
GBLK = 16
NBLK = T // GBLK
GJ = 8
NORM_EPS = 1e-6
GN_EPS = 64e-5
LAM_INIT = 0.8 - 0.6 * math.exp(-0.3)
N_MIX_IN = [26, 24]
STREAM = [("ada", 0, 48), ("mix_in", 0, N_MIX_IN[0]), ("ada", 1, 48), ("mix_out", 0, 8), ("query", 0, 16),
          ("peer", 0, 2 * NJ), ("mix_in", 1, N_MIX_IN[1]), ("mix_out", 1, 8), ("query", 1, 16), ("peer", 1, 2 * NJ)]
ADA_BLOCKS = 12
ADA1_EARLY = 9
LEVELS = 7
N_PARAM_LOADS = 3
UNITS = [(0, 0), (1, 0), (0, 1), (1, 2), (0, 2), (1, 1)]

N_FILLS = len(UNITS) * (3 + 10 + 6 * (LEVELS - 2) + 4 + 4) + 4

FEAT = {}
_at = 0
for _name, _n in [("w0", 8), ("a0", 8), ("k_k", 4), ("k_a", 4), ("r_k", 4), ("ln_g", 4), ("ln_b", 4),
                  ("conv", 12), ("norm_mix", 16), ("norm_ffn", 16), ("b_ada", 96), ("cond", 16), ("subln", 1), ("eps", 2)]:
    FEAT[_name] = _at
    _at += _n
N_FEAT = _at
CONST = {n: i for i, n in enumerate(["ident", "ones", "head_ones", "iota", "rot", "upper", "lower", "upper_eq",
                                     "lower_eq"])}
N_CONST = len(CONST)


def stage_tiles(layer):
    out, at = {}, 0
    for name, of, n in STREAM:
        if of == layer:
            out[name] = at
        at += n
    return out


def tile_kinds():
    kinds = []
    for name, layer, n in STREAM:
        if name == "peer":
            kinds += ["u"] * LAG + ["v"] * (2 * NJ - LAG)
        else:
            kinds += ["p" if name in ("mix_in", "query") else "d"] * n
    seen, out = {k: 0 for k in "dpuv"}, []
    for k in kinds:
        out.append((k, seen[k]))
        seen[k] += 1
    return out


HEAD_U = [0, 10, 20, 30, LAG]
TILES = tile_kinds()
SPLITS_BEFORE = [sum(k != "d" for k, _ in TILES[:g]) for g in range(len(TILES) + 1)]


def bc(ap, axis, n):
    a = ap.unsqueeze(axis)
    shape = list(a.shape)
    shape[axis] = n
    return a.broadcast_to(shape)


def build(nc, A):
    with ExitStack() as ctx:
        def sb(name, shape, dt=F32):
            return ctx.enter_context(nc.sbuf_tensor(name, shape, dt))

        def sb_at(name, shape, base, at, dt=F32R):
            return nc.alloc_sbuf_tensor_at(name, shape, dt, offset=base + 4 * at)

        def sem(name):
            return ctx.enter_context(nc.semaphore(name))

        ps = ctx.enter_context(nc.psum_tensor("ps", [P, 8, 512], F32))
        x = sb("x", [P, NT, D])
        ring = sb("ring", [P, RING, D])
        const = sb("const", [P, N_CONST, P])
        feats = sb("feats", [P, N_FEAT])
        silu_c = sb("silu_c", [P, DC, 2])
        mods = sb("mods", [P, 2, 48, 2])
        mod_scale = sb("mod_scale", [P, 2, 2, DC, 2])
        gate_bc = sb("gate_bc", [P, 2, D])
        xn = sb("xn", [P, NT, D])
        stat = sb("stat", [P, 96])
        hbase = nc.sbuf_base
        hslab = sb("hslab", [P, 2 * DC * T])
        abase = nc.sbuf_base
        arena = sb("arena", [P, 33024])
        assert hbase % 32 == 0 and abase - hbase == 8 * DC * T and nc.sbuf_base - abase == 4 * 33024
        hT_hi = sb_at("hT_hi", [P, DC, T], hbase, 0)
        hT_lo = sb_at("hT_lo", [P, DC, T], hbase, DC * T)
        g_dram = nc.dram_tensor("g_dram", [NBLK, P, P, GBLK], F32).ap()

        ident, ones, head_ones, iota, rot = (const[:, CONST[n], :] for n in ("ident", "ones", "head_ones", "iota", "rot"))

        def cm(name):
            return const[:, CONST[name], :]

        def ft(name, i=0, n=1):
            return feats[:, FEAT[name] + i:FEAT[name] + i + n]

        def area(at, *dims):
            n = 1
            for d_ in dims:
                n *= d_
            ap = arena[:, at:at + n]
            if len(dims) == 2:
                ap = ap.rearrange("p (a b) -> p a b", a=dims[0])
            elif len(dims) == 3:
                ap = ap.rearrange("p (a b c) -> p a b c", a=dims[0], b=dims[1])
            elif len(dims) == 4:
                ap = ap.rearrange("p (a b c d) -> p a b c d", a=dims[0], b=dims[1], c=dims[2])
            return ap

        hTf = hslab
        proj = area(0, 26, T)
        R_, K_, V_, WA, GD, BG, CG, HC = 0, 4, 8, 12, 13, 14, 18, 22
        YT_EVEN = 10
        dirv = [area(9984 + d * 6144, 4, NF, T) for d in range(2)]
        KAP, BET, GAM, RHO = range(4)
        lam = [area(22272 + d * 1536, NF, T) for d in range(2)]
        aa = [area(22272 + 3072 + d * 1536, NF, T) for d in range(2)]
        mat = area(22272, 2, 7, 4, P)
        ATM, AKM, RBM, RGM, XM, XTM, PM = range(7)
        kk = area(28416, NF, T)
        kdsum = area(29952, NF, T)
        rows = area(29440, 3, 512)
        rhs_s = area(29440 + 1536, 512)
        sa_s = area(29440 + 2048, 512)
        zst = [hTf[:, 2560 + d * 256:2816 + d * 256].rearrange("p (f v) -> p f v", f=NF) for d in range(2)]
        ada_row = area(31488, 2, 512)[0:2]
        ada_cols = ps[:, 7, 416:512].rearrange("p (n k) -> p n k", k=2)
        oT = proj[:, K_:K_ + NF, :]
        gT = proj[:, CG:CG + NF, :]
        qs = xn[:, :, :].rearrange("p a b -> p (a b)")[:, 0:1536].rearrange("p (f t) -> p f t", f=NF)
        ql = xn[:, :, :].rearrange("p a b -> p (a b)")[:, 1536:3072].rearrange("p (f t) -> p f t", f=NF)
        lvl = gate_bc[:, :, :].rearrange("p a b -> p (a b)")[:, 0:2 * LEVELS * P].rearrange("p (d l m) -> p d l m", d=2, l=LEVELS)
        half = [stat[:, 12 * d:12 * d + 12] for d in range(2)]
        dec = [stat[:, 24 + 12 * d:36 + 12 * d] for d in range(2)]
        omka = stat[:, 48:52]
        norm_ss = stat[:, 52:67]
        norm_std = stat[:, 67:82]
        lora = hTf[:, 0:1024].rearrange("p (d n) -> p d n", d=2)
        gup = hTf[:, 1024:1536]
        scan_mask = hTf[:, 1536:1536 + T]
        sfin = hTf[:, 2048:2560].rearrange("p (d f v) -> p d f v", d=2, f=NF)
        upd = area(0, 2, 512)
        nil = stat[:, 90:91]
        s0 = xn[:, :, :].rearrange("p a b -> p (a b)")[:, 0:512].rearrange("p (d f v) -> p d f v", d=2, f=NF)

        hT32 = area(16384, DC, T)

        qk = area(0, 16, T)
        vrow = area(6144, NT, D)
        ckT = area(9216, 8, P)
        cv = area(10240, D)
        orow = area(11264, NT, D)
        yT_odd = area(14336, DC, T)
        pe_ = area(17408, 2, 2, T)
        pT = area(18944, 2, NT, P)
        krow = area(19712, D)
        osq = area(20736, NT, D)
        lamv = area(23808, 256)
        ropet = area(24064, 2, 256)
        sm = area(24576, 2, 16)
        oss = area(24640, 24)
        lamc = area(24672, 4)
        ropec = area(24704, 2, 256)

        acts = area(0, LAG, T)
        qT = area(12288, 16, T)
        skT = area(18432, 16, P)
        selp = area(12288, 2, 1024)
        onehot = [area(12288 + 1024 * k, 2, 4, P) for k in range(4)]
        gstage = area(12288 + 4096, 2, P, GBLK)
        gtile = area(12288, 2, NBLK, GJ * GBLK)
        sc = [area(20480, 16, P), area(22528, 16, P), area(LAG * T - 2048, 16, P)]
        SC_SLOT = (LAG * T - 2048) // T
        selT = area(24576, 3, P)
        SM = 24960
        w_hi = sb_at("w_hi", [P, 2, D], abase, 26896)
        w_lo = sb_at("w_lo", [P, 2, D], abase, 26896 + 2 * D)
        ga_hi = sb_at("ga_hi", [P, 2, T], abase, 30992)
        ga_lo = sb_at("ga_lo", [P, 2, T], abase, 30992 + 2 * T)
        ga = xn[:, :, :].rearrange("p a b -> p (a b)")[:, 2048:2048 + 2 * T].rearrange("p (k t) -> p k t", k=2)
        sv = area(SM, 16, TOPK)
        si = area(SM + 256, 16, TOPK).bitcast(U32)
        sif = area(SM + 512, 16, TOPK)
        tv = area(SM + 768, NH, TOPK)
        ti = area(SM + 896, NH, TOPK).bitcast(U32)
        tab = area(SM + 1024, 2, 128).bitcast(U32)
        tabf = area(SM + 1280, 2, 128)
        sel3 = area(SM + 1536, 3, 128)
        gsum = area(SM + 1920, 2, 8)
        fin_g = area(20480, D)
        cand = xn[:, :, :].rearrange("p a b -> p (a b)")[:, 0:2048].rearrange("p (h c) -> p h c", h=NH)

        landed = [sem(f"weight_landed{i}") for i in range(RING)]
        multiplied = sem("multiplied")
        hi_ready = sem("hi_ready")
        lo_ready = {k: sem(f"lo_ready_{k}") for k in "puv"}
        h32_ready = sem("h32_ready")
        ga_f32 = sem("ga_f32")
        ga_high = sem("ga_high")
        params_in = sem("params_in")
        x_in = sem("x_in")
        state_in = sem("state_in")
        cond_sig = sem("cond_sig")
        silu_ready = sem("silu_ready")
        mods_ready = sem("mods_ready")
        ada_row_ready = sem("ada_row_ready")
        ada_cols_ready = sem("ada_cols_ready")
        x_updated = sem("x_updated")
        std_ready = sem("std_ready")
        xn_ready = sem("xn_ready")
        xT_ready = sem("xT_ready")
        hT_by_act = sem("hT_by_act")
        hT_by_dve = sem("hT_by_dve")
        proj_taken = sem("proj_taken")
        diag_ready = sem("diag_ready")
        gate_ready = sem("gate_ready")
        gate_taken = sem("gate_taken")
        conv_done = sem("conv_done")
        lora_act = sem("lora_act")
        lora_ready = sem("lora_ready")
        lora_taken = sem("lora_taken")
        ksq_ready = sem("ksq_ready")
        knorm_ready = sem("knorm_ready")
        knorm_root = sem("knorm_root")
        q_ready = sem("q_ready")
        exp_ready = sem("exp_ready")
        rkd_ready = sem("rkd_ready")
        bonus_ready = sem("bonus_ready")
        prep_done = sem("prep_done")
        fill_ready = sem("fill_ready")
        fill_taken = sem("fill_taken")
        state_ready = sem("state_ready")
        gn_ready = sem("gn_ready")
        gn_in = sem("gn_in")
        gn_root = sem("gn_root")
        y_even_ready = sem("y_even_ready")
        rot_ready = sem("rot_ready")
        rot_taken = sem("rot_taken")
        roped = sem("roped")
        v_ready = sem("v_ready")
        v_taken = sem("v_taken")
        krow_ps = sem("krow_ps")
        krow_ready = sem("krow_ready")
        caches_in = sem("caches_in")
        lam_sums = sem("lam_sums")
        lam_exp = sem("lam_exp")
        sc_ready = sem("sc_ready")
        mx_ready = sem("mx_ready")
        pexp_ready = sem("pexp_ready")
        attn_ready = sem("attn_ready")
        pT_ready = sem("pT_ready")
        pT_taken = sem("pT_taken")
        o_ready = sem("o_ready")
        o_taken = sem("o_taken")
        on_sums = sem("on_sums")
        on_root = sem("on_root")
        on_ready = sem("on_ready")
        oT_ready = sem("oT_ready")
        y_odd_ready = sem("y_odd_ready")
        lora_in = sem("lora_in")
        keys_in = sem("keys_in")
        fin_in = sem("fin_in")
        scores_ready = sem("scores_ready")
        scores_taken = sem("scores_taken")
        scores_used = sem("scores_used")
        gexp_in = sem("gexp_in")
        gexp_ready = sem("gexp_ready")
        sel_ready = sem("sel_ready")
        selT_ready = sem("selT_ready")
        selT_taken = sem("selT_taken")
        onehot_ready = sem("onehot_ready")
        onehot_gated = sem("onehot_gated")
        g_ready = sem("g_ready")
        g_taken = sem("g_taken")
        g_stored = [sem(f"g_stored{i}") for i in range(2)]
        g_in = [sem(f"g_in{i}") for i in range(2)]
        gelu_done = sem("gelu_done")
        ga_ready = sem("ga_ready")
        outs_done = sem("outs_done")
        onehots_read = sem("onehots_read")
        dve_order = sem("dve_order")
        act_order = sem("act_order")

        def mix_y(layer):
            return proj[:, YT_EVEN:YT_EVEN + DC, :] if layer == 0 else yT_odd

        block = ctx.enter_context(nc.Block())

        @block.sync
        def _(sp):
            sp.dma_start(feats[:, :], A["feats"]).then_inc(params_in, 16)
            sp.dma_start(const[:, :, :], A["const"]).then_inc(params_in, 16)
            sp.dma_start(x[:, 0, :], A["x_prompt"]).then_inc(x_in, 16)
            sp.dma_start(x[:, 1:3, :], A["x_sample"].rearrange("(t p) d -> p t d", p=P)).then_inc(x_in, 16)
            sp.dma_start(lvl, A["levels"]).then_inc(params_in, 16)

            def slot_free(g, it=None, step=0, turns=0):
                if it is None:
                    if g < RING:
                        return
                    kind, n = TILES[g - RING]
                    sp.wait_ge(multiplied if kind == "d" else lo_ready[kind], (g - RING if kind == "d" else n) + 1)
                    return
                kind, n1 = TILES[g + step - RING]
                value = [g + i * step - RING if kind == "d" else TILES[g + i * step - RING][1] for i in range(1, turns)]
                inc = value[1] - value[0] if turns > 2 else 0
                assert all(TILES[g + i * step - RING][0] == kind for i in range(1, turns))
                assert value == [value[0] + i * inc for i in range(turns - 1)]
                sp.wait_ge(multiplied if kind == "d" else lo_ready[kind], it * inc + (value[0] - inc + 1))

            def stream(g0, turns, parts):
                step = len(parts)

                def turn(i):
                    for k, (src, at, inc) in enumerate(parts):
                        g = g0 + k
                        if isinstance(i, int):
                            slot_free(g)
                            tile = src[at]
                        else:
                            slot_free(g, i, step, turns)
                            tile = src[bass.ds(i * inc + at, 1)].rearrange("a p n -> (a p) n")
                        sp.dma_start(ring[:, g % RING, :], tile).then_inc(landed[g % RING], 16)

                turn(0)
                if turns > 1:
                    with sp.Fori(1, turns) as i:
                        turn(i)

            def load_all(src, g0, n):
                turns = n // RING
                first = 0
                for m in range(1, turns):
                    if TILES[g0 + m * RING - RING][0] == TILES[g0 + m * RING - 1][0]:
                        first = m
                        break
                for m in range(first):
                    stream(g0 + m * RING, 1, [(src, m * RING + k, 0) for k in range(RING)])
                stream(g0 + first * RING, turns - first, [(src, first * RING + k, RING) for k in range(RING)])
                for k in range(turns * RING, n):
                    stream(g0 + k, 1, [(src, k, 0)])

            load_all(A["ada0"], stage_tiles(0)["ada"], 48)
            for layer in range(2):
                at = stage_tiles(layer)
                if layer == 0:
                    load_all(A["mix_in0"], at["mix_in"], 26)
                    load_all(A["ada1"], stage_tiles(1)["ada"], 48)
                else:
                    load_all(A["mix_in1"], at["mix_in"], 16)
                    load_all(A["mix_v1"], at["mix_in"] + 16, 8)
                load_all(A[f"mix_out{layer}"], at["mix_out"], 8)
                load_all(A[f"query{layer}"], at["query"], 16)
                g0 = at["peer"]
                u, v = A[f"u{layer}"], A[f"v{layer}"]
                load_all(u, g0, LAG)
                g0 += LAG
                stream(g0, (NJ - LAG) // 4, [p for k in range(4) for p in ((u, LAG + k, 4), (v, k, 4))])
                g0 += 2 * (NJ - LAG)
                load_all(v[NJ - LAG:NJ], g0, LAG)

        @block.tensor
        def _(pe):
            def tile_landed(g0, k, it=0):
                g = g0 + k
                pe.wait_ge(landed[g % RING], 16 * (g // RING + 1) + it * 16)
                return ring[:, g % RING, :].rearrange("p (c n) -> p c n", c=DC)

            def ada(layer, q0, q1):
                if layer == 0:
                    pe.wait_ge(silu_ready, 1)

                def to_columns(q):
                    pe.wait_ge(ada_row_ready, ADA_BLOCKS * layer + q + 1)
                    for c in range(4):
                        mm = pe.transpose(ada_cols[:, 4 * q + c, :], ada_row[:, q % 2, c * P:(c + 1) * P], ident[0:2, 0:2])
                    mm.then_inc(ada_cols_ready, 1)

                for q in range(q0, q1):
                    if q >= q0 + 3:
                        pe.wait_ge(ada_row_ready, ADA_BLOCKS * layer + q - 2)
                    for k in range(4):
                        w = tile_landed(stage_tiles(layer)["ada"], 4 * q + k).rearrange("p c n -> p (c n)")
                        for cc in range(2):
                            c = 2 * k + cc
                            mm = pe.matmul(ps[0:2, q % 3, :], silu_c[:, c, :], w[:, 512 * cc:512 * cc + 512],
                                           start=(c == 0), stop=(c == DC - 1))
                        mm.then_inc(multiplied, 1)
                    if q > q0:
                        to_columns(q - 1)
                to_columns(q1 - 1)

            def split_landed(g0, k, it=0, step=0):
                g = g0 + k
                kind, n = TILES[g]
                inc = sum(x == kind for x, _ in TILES[g:g + step]) if step else 0
                pe.wait_ge(lo_ready[kind], (n + 1) + it * inc)
                return w_hi[:, g % 2, :], w_lo[:, g % 2, :]

            def by_hT(out, w):
                hi, lo = (x.rearrange("p (c n) -> p c n", c=DC) for x in w)
                for c in range(DC):
                    pe.matmul(out, hi[:, c, :], hT_hi[:, c, :], start=(c == 0), stop=False)
                    pe.matmul(out, hi[:, c, :], hT_lo[:, c, :], start=False, stop=False)
                    mm = pe.matmul(out, lo[:, c, :], hT_hi[:, c, :], start=False, stop=(c == DC - 1))
                return mm

            def norm_T(n):
                if n == 0:
                    pe.wait_ge(params_in, 16 * N_PARAM_LOADS)
                for t in range(NT):
                    pe.wait_ge(xn_ready, NT * n + t + 1)
                    for hf in range(2):
                        for c in range(4):
                            mm = pe.transpose(ps[:, 2 * t + hf, c * P:(c + 1) * P],
                                              xn[:, t, (4 * hf + c) * P:(4 * hf + c + 1) * P], ident)
                        mm.then_inc(xT_ready, 1)
                pe.wait_ge(hT_by_act, NT * (n + 1))
                pe.wait_ge(hT_by_dve, NT * (n + 1))

            def project(g0, count, base, rotated=0):
                for n in range(count):
                    w = split_landed(g0, n)
                    if n >= 4:
                        pe.wait_ge(proj_taken, base + n - 3)
                    by_hT(ps[:, n % 4, 0:T], w).then_inc(multiplied, 1)
                    if 0 <= n - 2 < rotated:
                        rotate(base, n - 2)
                for n in range(count - 2, rotated):
                    rotate(base, n)

            def rotate(base, n):
                pe.wait_ge(proj_taken, base + n + 1)
                if n >= 2:
                    pe.wait_ge(rot_taken, n - 1)
                pe.matmul(ps[:, 6 + n % 2, 0:256], rot, qk[:, n, P:T], start=True, stop=True).then_inc(rot_ready, 1)

            def row_project_hT(g0):
                for nb in range(2):
                    for q in range(4):
                        hi, lo = (y.rearrange("p (c n) -> p c n", c=2) for y in split_landed(g0, nb * 4 + q))
                        for cc in range(2):
                            c = 2 * q + cc
                            for t in range(NT):
                                ts = slice(t * P, (t + 1) * P)
                                for m, (l_, r_) in enumerate(((hT_hi, hi), (hT_hi, lo), (hT_lo, hi))):
                                    mm = pe.matmul(ps[:, 3 * nb + t, :], l_[:, c, ts], r_[:, cc, :],
                                                   start=(c == 0 and m == 0), stop=(c == DC - 1 and m == 2))
                        mm.then_inc(multiplied, 1)

            def row_project(g0, act):
                for nb in range(2):
                    for q in range(4):
                        g = g0 + nb * 4 + q
                        pe.wait_ge(landed[g % RING], 16 * (g // RING + 1))
                        w = ring[:, g % RING, :].rearrange("p (c n) -> p c n", c=2)
                        for cc in range(2):
                            c = 2 * q + cc
                            for t in range(NT):
                                mm = pe.matmul(ps[:, 3 * nb + t, :], act[:, c, t * P:(t + 1) * P], w[:, cc, :],
                                               start=(c == 0), stop=(c == DC - 1))
                        mm.then_inc(multiplied, 1)

            def gate_rows(n):
                for q in range(4):
                    pe.wait_ge(diag_ready, 4 * n + q + 1)
                    if q >= 2:
                        pe.wait_ge(gate_taken, 4 * n + q - 1)
                    pe.matmul(ps[:, 6 + q % 2, :], ones, xn[:, 0:2, :].rearrange("p a b -> p (a b)")[:, 512 * q:512 * q + 512],
                              start=True, stop=True).then_inc(gate_ready, 1)

            def rwkv_prep():
                pe.wait_ge(lora_act, 2)
                pe.wait_ge(lora_in, 48)
                for m in range(20):
                    if m >= 4:
                        pe.wait_ge(lora_taken, m - 3)
                    if m < 16:
                        d, f, wa = m // 8, m % 4, (m // 4) % 2
                        k0 = HD * wa
                        mm = pe.matmul(ps[:, m % 4, 0:T], lora[k0:k0 + HD, d, f * P:(f + 1) * P],
                                       proj[k0:k0 + HD, WA, :], start=True, stop=True)
                    else:
                        f = m % 4
                        mm = pe.matmul(ps[:, m % 4, 0:T], gup[:, f * P:(f + 1) * P], proj[:, GD, :], start=True, stop=True)
                    mm.then_inc(lora_ready, 1)
                pe.wait_ge(ksq_ready, 1)
                for f in range(NF):
                    pe.matmul(ps[:, 4 + f, 0:T], head_ones, qs[:, f, :], start=True, stop=True).then_inc(knorm_ready, 1)
                pe.wait_ge(lora_taken, 20)
                pe.wait_ge(knorm_root, NF)
                ada(1, 0, ADA1_EARLY)
                pe.wait_ge(rkd_ready, 1)
                for f in range(NF):
                    pe.matmul(ps[:, 4 + f, 0:T], head_ones, qs[:, f, :], start=True, stop=True).then_inc(bonus_ready, 1)

            def rwkv_units():
                n = [0]

                def open_bank(need=None):
                    w = max(n[0] - 5, 0 if need is None else need + 1)
                    if w > 0:
                        pe.wait_ge(fill_taken, w)
                    b = n[0] % 6
                    n[0] += 1
                    return b

                pe.wait_ge(prep_done, 1)
                for q, (d, t) in enumerate(UNITS):
                    ts = slice(t * P, (t + 1) * P)
                    dv = dirv[d]
                    for src in (dv[:, BET], dv[:, GAM], proj[:, V_:V_ + NF]):
                        b = open_bank()
                        for f in range(NF):
                            mm = pe.transpose(ps[:, b, f * P:(f + 1) * P], src[:, f, ts], ident)
                        mm.then_inc(fill_ready, 1)

                    def head(h4, hf):
                        return h4, slice(HD * hf, HD * hf + HD)

                    for l_, r_ in ((BET, KAP), (KAP, BET), (GAM, KAP), (BET, RHO), (GAM, RHO)):
                        for hf in range(2):
                            b = open_bank()
                            for h4 in range(4):
                                f, kp = head(h4, hf)
                                mm = pe.matmul(ps[:, b, h4 * P:(h4 + 1) * P], dv[kp, l_, f, ts], dv[kp, r_, f, ts],
                                               start=True, stop=True)
                            mm.then_inc(fill_ready, 1)
                    base = n[0]
                    last_x = [base - 10 + 2, base - 10 + 3]
                    for lv in range(1, LEVELS):
                        p_at = n[0]
                        for hf in range(2):
                            b = open_bank(last_x[hf])
                            for h4 in range(4):
                                mm = pe.matmul(ps[:, b, h4 * P:(h4 + 1) * P], mat[:, hf, ATM, h4, :], mat[:, hf, XM, h4, :],
                                               start=True, stop=True)
                            mm.then_inc(fill_ready, 1)
                        if lv < LEVELS - 1:
                            last_x = [n[0], n[0] + 1]
                            for hf in range(2):
                                b = open_bank(p_at + hf)
                                for h4 in range(4):
                                    mm = pe.matmul(ps[:, b, h4 * P:(h4 + 1) * P], mat[:, hf, XTM, h4, :],
                                                   mat[:, hf, PM, h4, :], start=True, stop=True)
                                mm.then_inc(fill_ready, 1)
                            for hf in range(2):
                                b = open_bank(last_x[hf])
                                for h4 in range(4):
                                    mm = pe.transpose(ps[:, b, h4 * P:(h4 + 1) * P], mat[:, hf, XM, h4, :], ident)
                                mm.then_inc(fill_ready, 1)
                        else:
                            last_x = [n[0], n[0] + 1]
                            for hf in range(2):
                                b = open_bank(p_at + hf)
                                for h4 in range(4):
                                    mm = pe.matmul(ps[:, b, h4 * P:(h4 + 1) * P], mat[:, hf, PM, h4, :],
                                                   mat[:, hf, XTM, h4, :], start=True, stop=True)
                                mm.then_inc(fill_ready, 1)
                    if q in (2, 3):
                        pe.wait_ge(state_ready, q - 1)
                    for hf in range(2):
                        b = open_bank(last_x[1] if hf == 0 else None)
                        for h4 in range(4):
                            f, kp = head(h4, hf)
                            h = 2 * h4 + hf
                            o = ps[:, b, h4 * HD:(h4 + 1) * HD]
                            if t > 0:
                                pe.matmul(o, dv[kp, KAP, f, ts], zst[d][kp, f, :], start=True, stop=False)
                            mm = pe.matmul(o, mat[:, hf, AKM, h4, :], rows[:, 2, h * HD:(h + 1) * HD],
                                           start=(t == 0), stop=True)
                        mm.then_inc(fill_ready, 1)
                    b = open_bank(n[0] - 1)
                    for h in range(NH):
                        mm = pe.matmul(ps[:, b, h * HD:(h + 1) * HD], mat[:, h % 2, XTM, h // 2, :],
                                       rhs_s[:, h * HD:(h + 1) * HD], start=True, stop=True)
                    mm.then_inc(fill_ready, 1)
                    b = open_bank(n[0] - 1)
                    for h in range(NH):
                        f, kp = head(h // 2, h % 2)
                        o = ps[kp, b, f * P:(f + 1) * P]
                        hs = slice(h * HD, (h + 1) * HD)
                        if t > 0:
                            pe.matmul(o, zst[d][kp, f, :], dv[kp, RHO, f, ts], start=True, stop=False)
                        pe.matmul(o, rows[:, 2, hs], mat[:, h % 2, RGM, h // 2, :], start=(t == 0), stop=False)
                        mm = pe.matmul(o, sa_s[:, hs], mat[:, h % 2, RBM, h // 2, :], start=False, stop=True)
                    mm.then_inc(fill_ready, 1)
                    if q < 4:
                        b = open_bank()
                        for h in range(NH):
                            f, kp = head(h // 2, h % 2)
                            o = ps[kp, b, f * HD:(f + 1) * HD]
                            hs = slice(h * HD, (h + 1) * HD)
                            pe.matmul(o, rows[:, 0, hs], sa_s[:, hs], start=True, stop=False)
                            mm = pe.matmul(o, rows[:, 1, hs], rows[:, 2, hs], start=False, stop=True)
                        mm.then_inc(fill_ready, 1)

            def group_norm():
                pe.wait_ge(gn_in, 1)
                for f in range(NF):
                    pe.matmul(ps[:, f, 0:T], head_ones, oT[:, f, :], start=True, stop=True).then_inc(gn_ready, 1)
                pe.wait_ge(gn_in, 2)
                for f in range(NF):
                    pe.matmul(ps[:, 4 + f, 0:T], head_ones, kk[:, f, :], start=True, stop=True).then_inc(gn_ready, 1)
                pe.wait_ge(gn_root, NF)
                ada(1, ADA1_EARLY, ADA_BLOCKS)

            def attention():
                pe.wait_ge(v_taken, 6)
                pe.wait_ge(rot_taken, 16)
                for hf in range(2):
                    for c in range(4):
                        mm = pe.transpose(ps[:, 6 + hf, c * P:(c + 1) * P], qk[:, 8 + 4 * hf + c, 0:P], ident)
                    mm.then_inc(krow_ps, 1)
                pe.wait_ge(krow_ready, 2)
                pe.wait_ge(caches_in, 64)
                pe.wait_ge(roped, 16)
                units = [(t, h) for t in range(NT) for h in range(NH)]

                def scores(n):
                    t, h = units[n]
                    if n >= 2:
                        pe.wait_ge(pexp_ready, 2 * (n - 1))
                    for j in range(2):
                        kp = slice(HD * j, HD * j + HD)
                        o = ps[:, 2 * (n % 2) + j, :]
                        ql_ = qk[kp, h, t * P:(t + 1) * P]
                        if t == 0:
                            mm = pe.matmul(o[:, 0:P], ql_, qk[kp, 8 + h, 0:P], start=True, stop=True)
                        else:
                            pe.matmul(o[:, 0:256], ql_, qk[kp, 8 + h, P:T], start=True, stop=True)
                            mm = pe.matmul(o[:, 256:T], ql_, ckT[kp, h, :], start=True, stop=True)
                        mm.then_inc(sc_ready, 1)

                def weights_T(n):
                    t, h = units[n]
                    pe.wait_ge(attn_ready, n + 1)
                    if n >= 2:
                        pe.wait_ge(pT_taken, n - 1)
                    for b in range(1 if t == 0 else NT):
                        mm = pe.transpose(ps[:, 4 + n % 2, b * P:(b + 1) * P], pe_[:, n % 2, 0, b * P:(b + 1) * P], ident)
                    mm.then_inc(pT_ready, 1)

                def values(n):
                    t, h = units[n]
                    pe.wait_ge(pT_taken, n + 1)
                    if n >= 2:
                        pe.wait_ge(o_taken, n - 1)
                    kt = [0] if t == 0 else [1, 2, 3]
                    for q, b in enumerate(kt):
                        v = cv[:, h * P:(h + 1) * P] if b == 3 else vrow[:, b, h * P:(h + 1) * P]
                        mm = pe.matmul(ps[:, 6 + n % 2, 0:P], pT[:, n % 2, q, :], v, start=(q == 0), stop=(q == len(kt) - 1))
                    mm.then_inc(o_ready, 1)

                scores(0)
                scores(1)
                for n in range(24):
                    if n + 2 < 24:
                        scores(n + 2)
                    weights_T(n)
                    if n >= 1:
                        values(n - 1)
                values(23)
                for t in range(NT):
                    pe.wait_ge(on_ready, t + 1)
                    for hf in range(2):
                        for c in range(4):
                            mm = pe.transpose(ps[:, 2 * t + hf, c * P:(c + 1) * P],
                                              orow[:, t, (4 * hf + c) * P:(4 * hf + c + 1) * P], ident)
                        mm.then_inc(oT_ready, 1)

            def peer(layer):
                at = stage_tiles(layer)["peer"]
                pe.wait_ge(keys_in, 16 * (layer + 1))
                pe.wait_ge(gate_taken, 8 * (layer + 1))
                for t in range(NT):
                    for b in range(4):
                        n = 12 * layer + 4 * t + b
                        pe.wait_ge(proj_taken, proj_base(layer) + 16)
                        if t > 0:
                            pe.wait_ge(scores_taken, n - 3)
                        for c in range(4):
                            hj = 4 * b + c
                            mm = pe.matmul(ps[:, b, c * P:(c + 1) * P], qT[:, hj, t * P:(t + 1) * P], skT[:, hj, :],
                                           start=True, stop=True)
                        mm.then_inc(scores_ready, 1)

                def u_tile(g0, k, it, n0, step, first=False):
                    w = split_landed(g0[0], g0[1], it, 2 * step)
                    if not first:
                        pe.wait_ge(gelu_done, (n0 + k - 1) + it * step)
                    by_hT(ps[:, 6 + k % 2, 0:T], w).then_inc(multiplied, 1)

                U0 = NJ * layer
                for t in range(NT + 1):
                    for k in range(HEAD_U[t], HEAD_U[t + 1]):
                        u_tile((at, k), k, 0, U0, 0, first=(layer == 0 and k < 2))
                    if t == NT:
                        break
                    pe.wait_ge(sel_ready, NT * layer + t + 1)
                    pe.wait_ge(scores_taken, 12 * (layer + 1))
                    for w in range(3):
                        mm = pe.transpose(ps[:, 4, w * P:(w + 1) * P], sel3[:, w, :], ident)
                    mm.then_inc(selT_ready, 1)
                    G0 = 96 * layer + 32 * t

                    def gate_groups(g, first):
                        for k in range(4):
                            pe.wait_ge(onehot_gated, g + (k + 1))
                            if not first or k >= 2:
                                pe.wait_ge(g_taken, g + (k - 1))
                            for q in range(4):
                                mm = pe.matmul(ps[:, k % 2, q * P:(q + 1) * P], onehot[k][:, 0, q, :], onehot[k][:, 1, q, :],
                                               start=True, stop=True)
                            mm.then_inc(g_ready, 1)

                    gate_groups(G0, G0 == 0)
                    with pe.Fori(1, 8) as i:
                        gate_groups(i * 4 + G0, False)
                pe.wait_ge(g_taken, 96 * (layer + 1))

                def v_tile(g, n, it=0, step=0, first=False, last=False):
                    hi, lo = split_landed(g, 0, it, UNROLL if step else 0)
                    pe.wait_ge(ga_ready, (NJ * layer + n + 1) + it * step)
                    for t in range(NT):
                        for nb in range(2):
                            ts, cs = slice(t * P, (t + 1) * P), slice(nb * 512, (nb + 1) * 512)
                            for q, (l_, r_) in enumerate(((ga_hi, hi), (ga_hi, lo), (ga_lo, hi))):
                                mm = pe.matmul(ps[:, 2 * t + nb, :], l_[:, n % 2, ts], r_[:, cs],
                                               start=(first and q == 0), stop=(last and q == 2), skip_group_check=True)
                    mm.then_inc(multiplied, 1)

                g0 = at + LAG
                STEADY = (NJ - LAG) // 4
                for k in range(4):
                    u_tile((g0, 2 * k), k, 0, U0 + LAG, 0)
                    v_tile(g0 + 2 * k + 1, k, first=(k == 0))
                g0 += 8
                with pe.Fori(0, STEADY - 1) as i:
                    for k in range(4):
                        u_tile((g0, 2 * k), k, i, U0 + LAG + 4, 4)
                        v_tile(g0 + 2 * k + 1, 4 + k, i, 4)
                g0 += 8 * (STEADY - 1)
                n0 = NJ - LAG
                with pe.Fori(0, LAG // UNROLL - 1) as i:
                    for k in range(UNROLL):
                        v_tile(g0 + k, n0 + k, i, UNROLL)
                g0 += LAG - UNROLL
                n0 = NJ - UNROLL
                for k in range(UNROLL):
                    v_tile(g0 + k, n0 + k, last=(k == UNROLL - 1))

            def proj_base(layer):
                return 26 if layer == 0 else 26 + 16 + 16

            for layer in range(2):
                at = stage_tiles(layer)
                if layer:
                    pe.wait_ge(x_updated, 12)
                if layer == 0:
                    ada(0, 0, ADA_BLOCKS)
                norm_T(2 * layer)
                if layer == 0:
                    project(at["mix_in"], 26, 0)
                    pe.wait_ge(proj_taken, 26)
                    rwkv_prep()
                    rwkv_units()
                    group_norm()
                    pe.wait_ge(y_even_ready, 1)
                else:
                    project(at["mix_in"], 16, 42, rotated=16)
                    pe.wait_ge(proj_taken, 42 + 16)
                    row_project_hT(at["mix_in"] + 16)
                    attention()
                    pe.wait_ge(y_odd_ready, 6)
                gate_rows(2 * layer)
                row_project(at["mix_out"], mix_y(layer))
                norm_T(2 * layer + 1)
                project(at["query"], 16, proj_base(layer))
                gate_rows(2 * layer + 1)
                peer(layer)

        @block.scalar
        def _(act):
            order = [0]

            def chained(ins):
                order[0] += 1
                ins.then_inc(act_order, 1)
                act.wait_ge(act_order, order[0])

            def high(g, it=0, step=0):
                act.wait_ge(landed[g % RING], 16 * (g // RING + 1) + it * (16 * step // RING))
                if SPLITS_BEFORE[g] >= 2:
                    act.wait_ge(multiplied, (g - 1) + it * step)
                act.activation(w_hi[:, g % 2, :], ring[:, g % RING, :], ACT.Copy).then_inc(hi_ready, 1)

            def ada_rows(layer, q0, q1):
                for q in range(q0, q1):
                    act.wait_ge(multiplied, stage_tiles(layer)["ada"] + 4 * q + 4)
                    if ADA_BLOCKS * layer + q >= 2:
                        act.wait_ge(ada_cols_ready, ADA_BLOCKS * layer + q - 1)
                    act.activation(ada_row[:, q % 2, :], ps[0:2, q % 3, :], ACT.Copy).then_inc(ada_row_ready, 1)

            def norm_stats(n):
                for t in range(NT):
                    if n == 0:
                        act.wait_ge(x_in, 32)
                    else:
                        act.wait_ge(x_updated, 6 * (n - 1) + 3 + t + 1)
                    col = NT * n + t
                    chained(act.activation(xn[:, t, :], x[:, t, :], ACT.Square, accum_out=norm_ss[:, col:col + 1]))
                    act.activation(norm_std[:, col:col + 1], norm_ss[:, col:col + 1], ACT.Sqrt, scale=1.0 / D,
                                   bias=ft("eps", 0)).then_inc(std_ready, 1)

            def norm_evac(n):
                w, layer = n % 2, n // 2
                act.wait_ge(mods_ready, layer + 1)
                if n == 1:
                    act.wait_ge(outs_done, 32)
                for t in range(NT):
                    act.wait_ge(xT_ready, 6 * n + 2 * t + 1)
                    for c in range(4):
                        ins = act.activation(hT32[:, c, t * P:(t + 1) * P], ps[:, 2 * t, c * P:(c + 1) * P], ACT.Identity,
                                             bias=mods[:, layer, 24 * w + c, COND[t]:COND[t] + 1],
                                             scale=mod_scale[:, layer, w, c, COND[t]:COND[t] + 1])
                    ins.then_inc(h32_ready, 1)
                    act.wait_ge(h32_ready, NT * n + t + 1)
                    act.activation(hT_hi[:, 0:4, t * P:(t + 1) * P], hT32[:, 0:4, t * P:(t + 1) * P], ACT.Copy).then_inc(hT_by_act, 1)

            def take_projection(g0, count, dst, total):
                high(g0)
                high(g0 + 1)
                for n in range(count):
                    act.wait_ge(multiplied, g0 + n + 1)
                    if n + 2 < total:
                        high(g0 + n + 2)
                    act.activation(dst[:, n, :], ps[:, n % 4, 0:T], ACT.Copy).then_inc(proj_taken, 1)

            def rwkv_prep():
                act.wait_ge(proj_taken, 26)
                act.activation(proj[0:HD, WA, :], proj[0:HD, WA, :], ACT.Tanh).then_inc(lora_act, 1)
                act.activation(proj[:, GD, :], proj[:, GD, :], ACT.Sigmoid).then_inc(lora_act, 1)
                for m in range(20):
                    d, f, wa = m // 8, m % 4, (m // 4) % 2
                    act.wait_ge(lora_ready, m + 1)
                    if m == 16:
                        act.wait_ge(conv_done, 1)
                    if m < 16:
                        act.activation([lam, aa][wa][d][:, f, :], ps[:, m % 4, 0:T], ACT.Sigmoid,
                                       bias=ft(["w0", "a0"][wa], 4 * d + f)).then_inc(lora_taken, 1)
                    else:
                        act.activation(gT[:, f, :], ps[:, m % 4, 0:T], ACT.Copy).then_inc(lora_taken, 1)
                for f in range(NF):
                    act.wait_ge(knorm_ready, f + 1)
                    act.activation(ql[:, f, :], ps[:, 4 + f, 0:T], ACT.Sqrt).then_inc(knorm_root, 1)
                for d in range(2):
                    ada_rows(1, [0, 2][d], [2, 5][d])
                    act.wait_ge(q_ready, d + 1)
                    dv = dirv[d]
                    for dst, src, sg in (((RHO, qs, -1.0), (KAP, ql, -1.0), (GAM, qs, 1.0)) if d == 0 else
                                         ((RHO, ql, 1.0), (KAP, qs, 1.0), (GAM, ql, -1.0))):
                        act.activation(dv[:, dst], src, ACT.Exp, scale=sg).then_inc(exp_ready, 1)
                    act.activation(dec[d], half[d], ACT.Exp, scale=-1.0).then_inc(exp_ready, 1)
                ada_rows(1, 5, ADA1_EARLY)

            def group_norm():
                for f in range(NF):
                    act.wait_ge(gn_ready, NF + f + 1)
                    act.activation(qs[:, f, :], ps[:, 4 + f, 0:T], ACT.Sqrt, scale=1.0 / HD, bias=ft("eps", 1)).then_inc(gn_root, 1)
                ada_rows(1, ADA1_EARLY, ADA_BLOCKS)

            def attention():
                for n in range(6):
                    for m in ([18, 19, 20, 21] if n == 0 else [22, 23] if n == 3 else []):
                        high(stage_tiles(1)["mix_in"] + m)
                    act.wait_ge(multiplied, stage_tiles(1)["mix_in"] + 16 + 4 * (n // 3) + 4)
                    act.activation(vrow[:, n % 3, 512 * (n // 3):512 * (n // 3) + 512], ps[:, n, :], ACT.Copy).then_inc(v_taken, 1)
                for hf in range(2):
                    act.wait_ge(krow_ps, hf + 1)
                    act.activation(krow[:, hf * 512:(hf + 1) * 512], ps[:, 6 + hf, :], ACT.Copy).then_inc(krow_ready, 1)
                act.wait_ge(lam_sums, 2)
                act.activation(lamc[:, 2:4], lamc[:, 0:2], ACT.Exp).then_inc(lam_exp, 1)
                scale = HD ** -0.5

                def exps(n):
                    nk = P if n < NH else T
                    act.wait_ge(mx_ready, n + 1)
                    for j in range(2):
                        act.activation(pe_[:, n % 2, j, 0:nk], ps[:, 2 * (n % 2) + j, 0:nk], ACT.Exp,
                                       bias=sm[:, n % 2, j:j + 1], scale=scale,
                                       accum_out=sm[:, n % 2, 2 + j:3 + j]).then_inc(pexp_ready, 1)

                exps(0)
                exps(1)
                for n in range(24):
                    act.wait_ge(pT_ready, n + 1)
                    if n >= 2:
                        act.wait_ge(o_ready, n - 1)
                    nb = 1 if n < NH else NT
                    act.activation(pT[:, n % 2, 0:nb, :], ps[:, 4 + n % 2, 0:nb * P].rearrange("p (a b) -> p a b", a=nb),
                                   ACT.Copy).then_inc(pT_taken, 1)
                    if n + 2 < 24:
                        exps(n + 2)
                act.wait_ge(on_sums, 1)
                act.activation(oss, oss, ACT.Sqrt, scale=1.0 / P, bias=ft("eps", 0)).then_inc(on_root, 1)
                for b in range(6):
                    act.wait_ge(oT_ready, b + 1)
                    for c in range(4):
                        ins = act.activation(yT_odd[:, 4 * (b % 2) + c, (b // 2) * P:(b // 2 + 1) * P],
                                             ps[:, b, c * P:(c + 1) * P], ACT.Copy, scale=lamc[:, 3:4])
                    ins.then_inc(y_odd_ready, 1)

            def peer(layer):
                at = stage_tiles(layer)["peer"]
                for t in range(NT):
                    for b in range(4):
                        act.wait_ge(scores_ready, 12 * layer + 4 * t + b + 1)
                        act.activation(sc[t][:, 4 * b:4 * b + 4, :], ps[:, b, :].rearrange("p (a b) -> p a b", a=4),
                                       ACT.Copy).then_inc(scores_taken, 1)

                def store_block(b, blk):
                    act.dma_start(g_dram[bass.ds(blk, 1)].rearrange("a i j t -> (a i) (j t)"),
                                  gstage[:, b].rearrange("p j t -> p (j t)")).then_inc(g_stored[b], 16)

                def high_in(g, r, i2):
                    act.wait_ge(landed[g % RING], 16 * (g // RING + 1) + r * (16 * 64 // RING) + i2 * (16 * 32 // RING))
                    act.wait_ge(multiplied, (g - 1) + r * 64 + i2 * 32)
                    act.activation(w_hi[:, g % 2, :], ring[:, g % RING, :], ACT.Copy).then_inc(hi_ready, 1)

                def load_g(m, b):
                    act.dma_start(gtile[:, b], g_dram[:, :, bass.ds(m * GJ, GJ), :].rearrange("b i j t -> i b (j t)"))\
                       .then_inc(g_in[b], 16)

                high(at)
                high(at + 1)
                for t in range(NT + 1):
                    for k in range(HEAD_U[t], HEAD_U[t + 1]):
                        act.wait_ge(multiplied, at + k + 1)
                        high(at + k + 2)
                        if k == SC_SLOT:
                            act.wait_ge(scores_used, layer + 1)
                        act.activation(acts[:, k, :], ps[:, 6 + k % 2, 0:T], ACT.Gelu).then_inc(gelu_done, 1)
                    if t == NT:
                        break
                    act.wait_ge(gexp_in, NT * layer + t + 1)
                    act.activation(tv, tv, ACT.Exp).then_inc(gexp_ready, 1)
                    G0 = 96 * layer + 32 * t
                    S0 = 12 * layer + 4 * t

                    def blocks(i, first):
                        for b in range(2):
                            if not first:
                                act.wait_ge(g_stored[b], i * 16 + 16 * S0)
                            for q in range(4):
                                k = 4 * b + q
                                act.wait_ge(g_ready, (G0 + k + 1) + i * 8)
                                act.activation(gstage[:, b, :, 4 * q:4 * q + 4].rearrange("p j t -> p t j"),
                                               ps[:, k % 2, :].rearrange("p (t j) -> p t j", t=4), ACT.Copy)\
                                   .then_inc(g_taken, 1)
                            act.wait_ge(g_taken, (G0 + 4 * b + 4) + i * 8)
                            store_block(b, i * 2 + (8 * t + b))

                    blocks(0, S0 == 0)
                    with act.Fori(1, 4) as i:
                        blocks(i, False)
                for b in range(2):
                    act.wait_ge(g_stored[b], 16 * 12 * (layer + 1))
                act.wait_ge(onehots_read, layer + 1)
                load_g(0, 0)
                load_g(1, 1)
                with act.Fori(0, (NJ - LAG) // LAG) as r:
                    with act.Fori(0, 2) as i2:
                        for b in range(2):
                            for k in range(8):
                                j0 = 8 * b + k
                                act.wait_ge(multiplied, (at + LAG + 2 * j0 + 1) + r * (2 * LAG) + i2 * 32)
                                high_in(at + LAG + 2 * j0 + 2, r, i2)
                                act.wait_ge(ga_ready, (NJ * layer + j0 + 1) + r * LAG + i2 * 16)
                                act.activation(acts[:, bass.ds(i2 * 16 + j0, 1), :].rearrange("p a t -> p (a t)"),
                                               ps[:, 6 + k % 2, 0:T], ACT.Gelu).then_inc(gelu_done, 1)
                                high_in(at + LAG + 2 * j0 + 3, r, i2)
                            load_g(r * 4 + i2 * 2 + (b + 2), b)
                g0 = at + LAG + 2 * (NJ - LAG)
                for k in range(LAG - 2):
                    high(g0 + k + 2)
                    if k in (8, 16):
                        act.wait_ge(ga_ready, NJ * layer + (NJ - LAG) + k)
                        load_g(13 + k // 8, k // 8 - 1)

            act.wait_ge(params_in, 16 * N_PARAM_LOADS)
            act.activation(silu_c[:, :, :], ft("cond", 0, 16).rearrange("p (c k) -> p c k", k=2), ACT.Sigmoid).then_inc(cond_sig, 1)
            for layer in range(2):
                at = stage_tiles(layer)
                norm_stats(2 * layer)
                if layer == 0:
                    ada_rows(0, 0, ADA_BLOCKS)
                norm_evac(2 * layer)
                if layer == 0:
                    take_projection(at["mix_in"], 26, proj, 26)
                    rwkv_prep()
                    group_norm()
                else:
                    take_projection(at["mix_in"], 16, qk, 24)
                    attention()
                norm_stats(2 * layer + 1)
                norm_evac(2 * layer + 1)
                take_projection(at["query"], 16, qT, 16)
                peer(layer)
            norm_stats(4)

        @block.vector
        def _(dve):
            order = [0]

            def chained(ins):
                order[0] += 1
                ins.then_inc(dve_order, 1)
                dve.wait_ge(dve_order, order[0])

            def tt(out, a, b, op):
                return dve.tensor_tensor(out, a, b, op)

            def modulation(layer):
                dve.wait_ge(ada_cols_ready, ADA_BLOCKS * (layer + 1))
                ba = ft("b_ada", 48 * layer, 48)
                m = mods[:, layer]
                chained(tt(m, ada_cols, bc(ba, 2, 2), ALU.add))
                for w in range(2):
                    nw = ft("norm_mix" if w == 0 else "norm_ffn", 8 * layer, 8)
                    ins = dve.scalar_tensor_tensor(mod_scale[:, layer, w], m[:, 24 * w + 8:24 * w + 16, :], 1.0, bc(nw, 2, 2),
                                                   ALU.add, ALU.mult)
                    if w == 0:
                        chained(ins)
                ins.then_inc(mods_ready, 1)

            def normalise(n):
                for t in range(NT):
                    dve.wait_ge(std_ready, NT * n + t + 1)
                    col = NT * n + t
                    chained(dve.reciprocal(norm_std[:, col:col + 1], norm_std[:, col:col + 1]))
                    ins = dve.tensor_scalar(xn[:, t, :], x[:, t, :], norm_std[:, col:col + 1], None, ALU.mult)
                    if n == 4:
                        chained(ins)
                        if t == 0:
                            dve.wait_ge(fin_in, 16)
                        ins = tt(xn[:, t, :], xn[:, t, :], fin_g, ALU.mult)
                    ins.then_inc(xn_ready, 1)

            def norm_evac(n):
                w, layer = n % 2, n // 2
                dve.wait_ge(mods_ready, layer + 1)
                if n == 1:
                    dve.wait_ge(outs_done, 32)
                for t in range(NT):
                    dve.wait_ge(xT_ready, 6 * n + 2 * t + 2)
                    for c in range(4):
                        ins = dve.tensor_scalar(hT32[:, 4 + c, t * P:(t + 1) * P], ps[:, 2 * t + 1, c * P:(c + 1) * P],
                                                mod_scale[:, layer, w, 4 + c, COND[t]:COND[t] + 1],
                                                mods[:, layer, 24 * w + 4 + c, COND[t]:COND[t] + 1], ALU.mult, ALU.add)
                    chained(ins)
                    ts = slice(t * P, (t + 1) * P)
                    chained(dve.tensor_copy(hT_hi[:, 4:8, ts], hT32[:, 4:8, ts]))
                    tt(hT_lo[:, 4:8, ts], hT32[:, 4:8, ts], hT_hi[:, 4:8, ts].bitcast(F32), ALU.subtract)
                    dve.wait_ge(hT_by_act, NT * n + t + 1)
                    tt(hT_lo[:, 0:4, ts], hT32[:, 0:4, ts], hT_hi[:, 0:4, ts].bitcast(F32), ALU.subtract).then_inc(hT_by_dve, 1)

            def gate_rows(n):
                xf = xn[:, :, :].rearrange("p a b -> p (a b)")
                w, layer = n % 2, n // 2
                for q in range(4):
                    for c4 in range(4):
                        m = 4 * q + c4
                        ins = dve.tensor_scalar(xf[:, m * P:(m + 1) * P], ident,
                                                mods[:, layer, 24 * w + 16 + m % 8, m // 8:m // 8 + 1], None, ALU.mult)
                    ins.then_inc(diag_ready, 1)
                for q in range(4):
                    dve.wait_ge(gate_ready, 4 * n + q + 1)
                    dve.tensor_copy(gate_bc[:, q // 2, 512 * (q % 2):512 * (q % 2) + 512], ps[:, 6 + q % 2, :]).then_inc(gate_taken, 1)

            def residual(n, bank, ready):
                dve.wait_ge(gate_taken, 4 * (n + 1))
                for nb in range(2):
                    dve.wait_ge(multiplied, ready[nb])
                    for t in range(NT):
                        cols = slice(512 * nb, 512 * nb + 512)
                        tmp = upd[:, (NT * nb + t) % 2, :]
                        if NT * nb + t >= 2:
                            dve.wait_ge(x_updated, 6 * n + NT * nb + t - 1)
                        chained(tt(tmp, ps[:, bank(nb, t), :], gate_bc[:, COND[t], cols], ALU.mult))
                        tt(x[:, t, cols], x[:, t, cols], tmp, ALU.add).then_inc(x_updated, 1)

            def low(g, it=0, inc=0, per=0):
                dve.wait_ge(hi_ready, (SPLITS_BEFORE[g] + 1) + it * inc)
                tt(w_lo[:, g % 2, :], ring[:, g % RING, :], w_hi[:, g % 2, :].bitcast(F32), ALU.subtract)\
                    .then_inc(lo_ready[TILES[g][0]], 1)

            def short_conv():
                dve.wait_ge(proj_taken, 26)
                z, y = proj[:, CG:CG + NF, :], proj[:, HC:HC + NF, :]
                chained(tt(z, z, y, ALU.mult))
                for f in range(NF):
                    ins = dve.tensor_scalar(y[:, f, :], z[:, f, :], ft("conv", 4 + f), None, ALU.mult)
                chained(ins)
                for w, lo in ((0, 1), (8, 0)):
                    for f in range(NF):
                        for a, b in ((0, P), (P, T)):
                            out = y[:, f, a + 1:b] if lo else y[:, f, a:b - 1]
                            src = z[:, f, a:b - 1] if lo else z[:, f, a + 1:b]
                            ins = dve.scalar_tensor_tensor(out, src, ft("conv", w + f), out, ALU.mult, ALU.add)
                    chained(ins)
                tt(proj[:, BG:BG + NF, :], proj[:, BG:BG + NF, :], y, ALU.mult).then_inc(conv_done, 1)

            def rwkv_prep():
                for f in range(NF):
                    ins = dve.tensor_scalar(kk[:, f, :], proj[:, K_ + f, :], ft("k_k", f), None, ALU.mult)
                chained(ins)
                tt(qs, kk, kk, ALU.mult).then_inc(ksq_ready, 1)
                chained(dve.tensor_scalar(omka, ft("k_a", 0, 4), -1.0, 1.0, ALU.mult, ALU.add))
                dve.wait_ge(knorm_root, NF)
                chained(dve.tensor_scalar(ql, ql, 1e-12, None, ALU.max))
                chained(dve.reciprocal(ql, ql))
                chained(tt(kk, kk, ql, ALU.mult))
                dve.wait_ge(lora_in, 48)
                for d in range(2):
                    dv = dirv[d]
                    dve.wait_ge(lora_taken, 8 * d + 8)
                    chained(dve.tensor_scalar(lam[d], lam[d], math.exp(-0.5), None, ALU.mult))
                    for f in range(NF):
                        ins = dve.tensor_tensor_scan(qs[:, f, :], scan_mask, lam[d][:, f, :], 0.0, ALU.mult, ALU.add)
                    chained(ins)
                    q4 = qs.rearrange("p f (t m) -> p (f t) m", t=NT)
                    chained(dve.tensor_scalar(half[d], q4[:, :, P - 1], 0.5, None, ALU.mult))
                    chained(tt(q4, q4, bc(half[d], 2, P), ALU.subtract))
                    chained(tt(ql, qs, lam[d], ALU.subtract))
                    dve.tensor_copy(nil, half[d][:, 0:1]).then_inc(q_ready, 1)
                    for f in range(NF):
                        ins = dve.tensor_scalar(lam[d][:, f, :], aa[d][:, f, :], ft("k_a", f), omka[:, f:f + 1], ALU.mult, ALU.add)
                    chained(ins)
                    chained(tt(lam[d], lam[d], proj[:, K_:K_ + NF, :], ALU.mult))
                    if d == 0:
                        dve.tensor_copy(kdsum, lam[d])
                    else:
                        tt(kdsum, kdsum, lam[d], ALU.add)
                    chained(tt(aa[d], aa[d], kk, ALU.mult))
                    dve.wait_ge(exp_ready, 4 * d + 4)
                    chained(tt(dv[:, BET], aa[d], dv[:, GAM], ALU.mult))
                    tt(dv[:, GAM], dv[:, GAM], lam[d], ALU.mult)
                    tt(dv[:, RHO], dv[:, RHO], proj[:, R_:R_ + NF, :], ALU.mult)
                    chained(tt(dv[:, KAP], dv[:, KAP], kk, ALU.mult))
                chained(tt(qs, kdsum, proj[:, R_:R_ + NF, :], ALU.mult))
                for f in range(NF):
                    ins = dve.tensor_scalar(qs[:, f, :], qs[:, f, :], ft("r_k", f), None, ALU.mult)
                ins.then_inc(rkd_ready, 1)
                for f in range(NF):
                    dve.wait_ge(bonus_ready, f + 1)
                    ins = tt(proj[:, R_ + f, :], ps[:, 4 + f, 0:T], proj[:, V_ + f, :], ALU.mult)
                dve.wait_ge(lora_taken, 20)
                ins.then_inc(prep_done, 1)

            def rwkv_units():
                n = [0]

                def filled():
                    dve.wait_ge(fill_ready, n[0] + 1)
                    b = n[0] % 6
                    n[0] += 1
                    return ps[:, b, :]

                def four(ap):
                    return ap.rearrange("p (h m) -> p h m", h=4)

                dve.wait_ge(prep_done, 1)
                for q, (d, t) in enumerate(UNITS):
                    strict_T, strict, incl = [("upper", "lower", "upper_eq"), ("lower", "upper", "lower_eq")][d]
                    for w in range(3):
                        dve.tensor_copy(rows[:, w, :], filled()).then_inc(fill_taken, 1)
                    for hf in range(2):
                        b = four(filled())
                        chained(tt(mat[:, hf, ATM], b, bc(cm(strict_T), 1, 4), ALU.mult))
                        chained(tt(mat[:, hf, XTM], mat[:, hf, ATM], bc(lvl[:, 1 - d, 0, :], 1, 4), ALU.mult))
                        tt(mat[:, hf, XTM], bc(ident, 1, 4), mat[:, hf, XTM], ALU.subtract).then_inc(fill_taken, 1)
                    for hf in range(2):
                        b = four(filled())
                        chained(tt(mat[:, hf, XM], b, bc(lvl[:, d, 0, :], 1, 4), ALU.mult))
                        tt(mat[:, hf, XM], bc(ident, 1, 4), mat[:, hf, XM], ALU.subtract).then_inc(fill_taken, 1)
                    for which, mask in ((AKM, strict_T), (RBM, incl), (RGM, incl)):
                        for hf in range(2):
                            tt(mat[:, hf, which], four(filled()), bc(cm(mask), 1, 4), ALU.mult).then_inc(fill_taken, 1)
                    for lv in range(1, LEVELS):
                        for hf in range(2):
                            tt(mat[:, hf, PM], four(filled()), bc(lvl[:, d, lv, :], 1, 4), ALU.mult).then_inc(fill_taken, 1)
                        which = XM if lv < LEVELS - 1 else XTM
                        for hf in range(2):
                            tt(mat[:, hf, which], mat[:, hf, which], four(filled()), ALU.subtract).then_inc(fill_taken, 1)
                        if lv < LEVELS - 1:
                            for hf in range(2):
                                dve.tensor_copy(mat[:, hf, XTM], four(filled())).then_inc(fill_taken, 1)
                    for hf in range(2):
                        dve.tensor_copy(rhs_s.rearrange("p (h two v) -> p h two v", two=2, v=HD)[:, :, hf, :],
                                        filled()[:, 0:256].rearrange("p (h v) -> p h v", h=4)).then_inc(fill_taken, 1)
                    dve.tensor_scalar(sa_s, filled(), -1.0, None, ALU.mult).then_inc(fill_taken, 1)
                    ot = oT[:, :, t * P:(t + 1) * P]
                    y = four(filled())
                    if q in (0, 2, 3):
                        dve.tensor_copy(ot, y).then_inc(fill_taken, 1)
                    else:
                        tt(ot, ot, y, ALU.add).then_inc(fill_taken, 1)
                    if q < 4:
                        s = filled()[:, 0:NF * HD].rearrange("p (f v) -> p f v", f=NF)
                        g = dec[d].rearrange("p (f t) -> p f t", t=NT)
                        if q < 2:
                            dve.tensor_tensor(zst[d], s, bc(g[:, :, t], 2, HD), ALU.mult).then_inc(fill_taken, 1)
                            dve.wait_ge(fill_taken, n[0])
                            chained(dve.tensor_copy(sfin[:, d], zst[d]))
                            dve.wait_ge(state_in, 16)
                            t1 = 1 if d == 0 else 2
                            tt(zst[d], s0[:, d], bc(g[:, :, t1], 2, HD), ALU.mult).then_inc(state_ready, 1)
                        else:
                            tn = 2 if d == 0 else 1
                            chained(tt(zst[d], zst[d], s, ALU.add))
                            chained(tt(zst[d], zst[d], bc(g[:, :, t], 2, HD), ALU.mult))
                            tt(zst[d], zst[d], bc(g[:, :, tn], 2, HD), ALU.mult).then_inc(fill_taken, 1)

            def group_norm():
                dve.wait_ge(fill_taken, N_FILLS)
                dve.tensor_copy(nil, half[0][:, 0:1]).then_inc(gn_in, 1)
                for f in range(NF):
                    dve.wait_ge(gn_ready, f + 1)
                    ins = dve.scalar_tensor_tensor(oT[:, f, :], ps[:, f, 0:T], -1.0 / HD, oT[:, f, :], ALU.mult, ALU.add)
                chained(ins)
                tt(kk, oT, oT, ALU.mult).then_inc(gn_in, 1)
                dve.wait_ge(gn_root, NF)
                chained(dve.reciprocal(qs, qs))
                chained(tt(oT, oT, qs, ALU.mult))
                for f in range(NF):
                    ins = dve.tensor_scalar(oT[:, f, :], oT[:, f, :], ft("ln_g", f), ft("ln_b", f), ALU.mult, ALU.add)
                chained(ins)
                chained(tt(oT, oT, proj[:, R_:R_ + NF, :], ALU.add))
                tt(proj[:, YT_EVEN:YT_EVEN + NF, :], oT, gT, ALU.mult).then_inc(y_even_ready, 1)

            def rope(m):
                if m == 0:
                    dve.wait_ge(caches_in, 64)
                dve.wait_ge(rot_ready, m + 1)
                r = ropet[:, m % 2, :]
                xq = qk[:, m, P:T]
                if m >= 2:
                    dve.wait_ge(roped, m - 1)
                dve.tensor_tensor(r, ps[:, 6 + m % 2, 0:256], ropec[:, 1, :], ALU.mult).then_inc(rot_taken, 1)
                chained(tt(xq, xq, ropec[:, 0, :], ALU.mult))
                dve.wait_ge(rot_taken, m + 1)
                tt(xq, xq, r, ALU.add).then_inc(roped, 1)

            def attention():
                for i in range(2):
                    a = lamv[:, 128 * i:128 * i + 64]
                    b = lamv[:, 128 * i + 64:128 * i + 128]
                    dve.tensor_tensor_reduce(osq[:, 0, 0:64], a, b, 1.0, 0.0, ALU.mult, ALU.add, lamc[:, i:i + 1]).then_inc(lam_sums, 1)
                    dve.wait_ge(lam_sums, i + 1)
                dve.wait_ge(lam_exp, 1)
                chained(tt(lamc[:, 0:1], lamc[:, 3:4], lamc[:, 2:3], ALU.subtract))
                chained(dve.tensor_scalar(lamc[:, 0:1], lamc[:, 0:1], -LAM_INIT, None, ALU.add))
                chained(dve.tensor_scalar(lamc[:, 3:4], ft("subln"), 1.0 - LAM_INIT, None, ALU.mult))
                scale = HD ** -0.5

                def maxes(n):
                    nk = P if n < NH else T
                    s = sm[:, n % 2, :]
                    dve.wait_ge(sc_ready, 2 * n + 2)
                    chained(dve.tensor_reduce(s[:, 0:2], ps[:, 2 * (n % 2):2 * (n % 2) + 2, 0:nk], AX_X, ALU.max))
                    dve.tensor_scalar(s[:, 0:2], s[:, 0:2], -scale, None, ALU.mult).then_inc(mx_ready, 1)

                def take_o(n):
                    t, h = n // NH, n % NH
                    dve.wait_ge(o_ready, n + 1)
                    dve.tensor_copy(orow[:, t, h * P:(h + 1) * P], ps[:, 6 + n % 2, 0:P]).then_inc(o_taken, 1)

                maxes(0)
                maxes(1)
                for n in range(24):
                    nk = P if n < NH else T
                    s = sm[:, n % 2, :]
                    dve.wait_ge(pexp_ready, 2 * n + 2)
                    chained(dve.reciprocal(s[:, 4:6], s[:, 2:4]))
                    chained(tt(s[:, 6:7], s[:, 5:6], lamc[:, 0:1], ALU.mult))
                    chained(dve.tensor_scalar(pe_[:, n % 2, 1, 0:nk], pe_[:, n % 2, 1, 0:nk], s[:, 6:7], None, ALU.mult))
                    dve.scalar_tensor_tensor(pe_[:, n % 2, 0, 0:nk], pe_[:, n % 2, 0, 0:nk], s[:, 4:5],
                                             pe_[:, n % 2, 1, 0:nk], ALU.mult, ALU.add).then_inc(attn_ready, 1)
                    if n + 2 < 24:
                        maxes(n + 2)
                    if n >= 2:
                        take_o(n - 2)
                take_o(22)
                take_o(23)
                dve.wait_ge(o_taken, 24)
                chained(tt(osq, orow, orow, ALU.mult))
                dve.tensor_reduce(oss, osq.rearrange("p t (h e) -> p (t h) e", h=NH), AX_X, ALU.add).then_inc(on_sums, 1)
                dve.wait_ge(on_root, 1)
                chained(dve.reciprocal(oss, oss))
                for t in range(NT):
                    o3 = orow[:, t, :].rearrange("p (h e) -> p h e", h=NH)
                    tt(o3, o3, bc(oss[:, NH * t:NH * t + NH], 2, P), ALU.mult).then_inc(on_ready, 1)

            def rank(layer, t):
                s = sc[t]
                for r in range(2):
                    lo = slice(8 * r, 8 * r + 8)
                    for hj in range(16):
                        ins = dve.max(sv[:, hj, lo], s[:, hj, :])
                    chained(ins)
                    for hj in range(16):
                        ins = dve.max_index(si[:, hj, lo], sv[:, hj, lo], s[:, hj, :])
                    if r == 0:
                        for hj in range(16):
                            ins = dve.match_replace(s[:, hj, :], sv[:, hj, lo], s[:, hj, :], -3.0e38)
                    chained(ins)
                if t == NT - 1:
                    dve.tensor_copy(nil, sv[:, 0, 0:1]).then_inc(scores_used, 1)
                chained(dve.tensor_copy(sif, si))
                sv4 = sv.rearrange("p (h j) k -> p h j k", j=2)
                chained(tt(cand.rearrange("p h (a b) -> p h a b", a=TOPK), bc(sv4[:, :, 0, :], 3, TOPK),
                           bc(sv4[:, :, 1, :], 2, TOPK), ALU.add))
                for r in range(2):
                    lo = slice(8 * r, 8 * r + 8)
                    for h in range(NH):
                        ins = dve.max(tv[:, h, lo], cand[:, h, :])
                    chained(ins)
                    for h in range(NH):
                        ins = dve.max_index(ti[:, h, lo], tv[:, h, lo], cand[:, h, :])
                    if r == 0:
                        for h in range(NH):
                            ins = dve.match_replace(cand[:, h, :], tv[:, h, lo], cand[:, h, :], -3.0e38)
                    chained(ins)
                chained(dve.tensor_copy(gsum[:, 1, :], tv[:, :, 0]))
                tt(tv, tv, bc(gsum[:, 1, :], 2, TOPK), ALU.subtract).then_inc(gexp_in, 1)
                tif = ti.rearrange("p h k -> p (h k)")
                dve.tensor_scalar(tab[:, 0, :], tif, 4, None, ALU.logical_shift_right)
                chained(dve.tensor_scalar(tab[:, 1, :], tif, 15, None, ALU.bitwise_and))
                chained(dve.tensor_copy(tabf, tab))
                sif4 = sif.rearrange("p (h j) k -> p h j k", j=2)
                if t > 0:
                    dve.wait_ge(g_ready, 96 * layer + 32 * t)
                for w in range(2):
                    for hh in range(2):
                        eq = selp[:, 0].rearrange("p (m a) -> p m a", a=TOPK)
                        pr = selp[:, 1].rearrange("p (m a) -> p m a", a=TOPK)
                        ab = tabf[:, w, 64 * hh:64 * hh + 64]
                        chained(tt(eq, bc(ab, 2, TOPK), bc(iota[:, 0:TOPK], 1, 64), ALU.is_equal))
                        src = bc(sif4[:, 4 * hh:4 * hh + 4, w, :], 2, TOPK)
                        chained(tt(pr.rearrange("p (h k) a -> p h k a", h=4), eq.rearrange("p (h k) a -> p h k a", h=4), src, ALU.mult))
                        chained(dve.tensor_reduce(sel3[:, w, 64 * hh:64 * hh + 64], pr, AX_X, ALU.add))
                dve.wait_ge(gexp_ready, NT * layer + t + 1)
                chained(dve.tensor_reduce(gsum[:, 0, :], tv, AX_X, ALU.add))
                chained(dve.reciprocal(gsum[:, 0, :], gsum[:, 0, :]))
                tt(sel3[:, 2, :].rearrange("p (h k) -> p h k", h=NH), tv, bc(gsum[:, 0, :], 2, TOPK), ALU.mult).then_inc(sel_ready, 1)
                dve.wait_ge(selT_ready, NT * layer + t + 1)
                dve.tensor_copy(selT, ps[:, 4, 0:3 * P].rearrange("p (w t) -> p w t", w=3)).then_inc(selT_taken, 1)
                dve.wait_ge(selT_taken, NT * layer + t + 1)

            def spread(layer, t):
                G0 = 96 * layer + 32 * t

                def groups(i, first):
                    for k in range(4):
                        if not first:
                            dve.wait_ge(g_ready, i * 4 + (G0 + k - 3))
                        tt(onehot[k], iota.unsqueeze(1).unsqueeze(1).broadcast_to([P, 2, 4, P]),
                           bc(selT[:, 0:2, bass.ds(i * 16 + 4 * k, 4)], 3, P), ALU.is_equal).then_inc(onehot_ready, 1)

                groups(0, G0 == 0)
                with dve.Fori(1, 8) as i:
                    groups(i, False)

            def peer(layer):
                dve.wait_ge(scores_taken, 12 * (layer + 1))
                for t in range(NT):
                    rank(layer, t)
                    spread(layer, t)
                dve.wait_ge(g_ready, 96 * (layer + 1))
                dve.tensor_copy(nil, norm_std[:, 0:1]).then_inc(onehots_read, 1)
                at = stage_tiles(layer)["peer"]

                def gated(j0, g, i2, r):
                    b, k, js = (j0 % 16) // 8, j0 % 8, j0 % 32
                    tr, ti = (64, 32) if r is not None else (0, 16)
                    r = 0 if r is None else r
                    n = NJ * layer + j0
                    if ti == 32:
                        dve.wait_ge(hi_ready, SPLITS_BEFORE[g] + r * tr + i2 * ti)
                        tt(w_lo[:, (g - 1) % 2, :], ring[:, (g - 1) % RING, :], w_hi[:, (g - 1) % 2, :].bitcast(F32),
                           ALU.subtract).then_inc(lo_ready["v"], 1)
                    if k == 0:
                        dve.wait_ge(g_in[b], 16 * (8 * layer + 1 + 2 * (j0 // 32)) + i2 * 16 + r * 32)
                    dve.wait_ge(gelu_done, (n + 1) + r * LAG + i2 * 16)
                    if layer or j0 >= 2:
                        dve.wait_ge(ga_ready, (n - 1) + r * LAG + i2 * 16)
                    tt(ga[:, k % 2, :].rearrange("p (b t) -> p b t", t=GBLK),
                       acts[:, bass.ds(i2 * 16 + js, 1), :].rearrange("p a (b t) -> p (a b) t", t=GBLK),
                       gtile[:, b, :, GBLK * k:GBLK * (k + 1)], ALU.mult).then_inc(ga_f32, 1)
                    dve.wait_ge(multiplied, (back_count(j0, g, ti)) + r * tr + i2 * ti)
                    dve.wait_ge(ga_f32, (n + 1) + r * LAG + i2 * 16)
                    dve.tensor_copy(ga_hi[:, k % 2, :], ga[:, k % 2, :]).then_inc(ga_high, 1)
                    dve.wait_ge(ga_high, (n + 1) + r * LAG + i2 * 16)
                    tt(ga_lo[:, k % 2, :], ga[:, k % 2, :], ga_hi[:, k % 2, :].bitcast(F32), ALU.subtract).then_inc(ga_ready, 1)
                    dve.wait_ge(hi_ready, (SPLITS_BEFORE[g] + 1) + r * tr + i2 * ti)
                    tt(w_lo[:, g % 2, :], ring[:, g % RING, :], w_hi[:, g % 2, :].bitcast(F32), ALU.subtract)\
                        .then_inc(lo_ready["v"], 1)

                def back_count(j0, g, ti):
                    return g - 3 if ti == 32 else g - 1

                with dve.Fori(0, (NJ - LAG) // LAG) as r:
                    with dve.Fori(0, 2) as i2:
                        for j0 in range(16):
                            gated(j0, at + LAG + 2 * j0 + 1, i2, r)
                with dve.Fori(0, 2) as i2:
                    for j0 in range(16):
                        gated(NJ - LAG + j0, at + LAG + 2 * (NJ - LAG) + j0, i2, None)

            dve.wait_ge(params_in, 16 * N_PARAM_LOADS)
            dve.wait_ge(cond_sig, 1)
            tt(silu_c[:, :, :], silu_c[:, :, :], ft("cond", 0, 16).rearrange("p (c k) -> p c k", k=2), ALU.mult).then_inc(silu_ready, 1)
            for layer in range(2):
                at = stage_tiles(layer)
                normalise(2 * layer)
                if layer == 0:
                    modulation(0)
                norm_evac(2 * layer)
                for n in range(N_MIX_IN[layer]):
                    low(at["mix_in"] + n)
                    if layer == 1 and 4 <= n < 20:
                        rope(n - 4)
                if layer == 0:
                    short_conv()
                    rwkv_prep()
                    rwkv_units()
                    group_norm()
                    modulation(1)
                else:
                    attention()
                gate_rows(2 * layer)
                mo = at["mix_out"]
                residual(2 * layer, lambda nb, t: 3 * nb + t, (mo + 4, mo + 8))
                normalise(2 * layer + 1)
                norm_evac(2 * layer + 1)
                for n in range(16):
                    low(at["query"] + n)
                gate_rows(2 * layer + 1)
                peer(layer)
                end = at["peer"] + 2 * NJ
                residual(2 * layer + 1, lambda nb, t: 2 * t + nb, (end, end))
            normalise(4)

        @block.gpsimd
        def _(pool):
            def u_low(layer, k0, k1):
                for k in range(k0, k1):
                    g = stage_tiles(layer)["peer"] + k
                    pool.wait_ge(hi_ready, SPLITS_BEFORE[g] + 1)
                    pool.tensor_tensor(w_lo[:, g % 2, :], ring[:, g % RING, :], w_hi[:, g % 2, :].bitcast(F32),
                                       ALU.subtract).then_inc(lo_ready["u"], 1)

            def gate_onehots(layer, t):
                G0 = 96 * layer + 32 * t
                with pool.Fori(0, 8) as i:
                    for k in range(4):
                        pool.wait_ge(onehot_ready, i * 4 + (G0 + k + 1))
                        pool.tensor_tensor(onehot[k][:, 1], onehot[k][:, 1], bc(selT[:, 2, bass.ds(i * 16 + 4 * k, 4)], 2, P),
                                           ALU.mult).then_inc(onehot_gated, 1)

            def peer_head(layer):
                low_done = [0] + [min(n + 2, LAG) for n in HEAD_U[1:NT + 1]]
                for t in range(NT):
                    u_low(layer, low_done[t], low_done[t + 1])
                    gate_onehots(layer, t)
                u_low(layer, low_done[NT], LAG)

            pool.wait_ge(multiplied, stage_tiles(0)["mix_in"] + 26)
            pool.dma_start(lora, A["lora"]).then_inc(lora_in, 16)
            pool.dma_start(gup, A["gup"]).then_inc(lora_in, 16)
            pool.dma_start(scan_mask, A["scan_mask"]).then_inc(lora_in, 16)
            pool.wait_ge(prep_done, 1)
            pool.dma_start(s0, A["state"]).then_inc(state_in, 16)
            for d in range(2):
                pool.wait_ge(state_ready, d + 1)
                pool.dma_start(A["out_state"][d], sfin[:, d]).then_inc(outs_done, 16)
            pool.wait_ge(hT_by_dve, 2 * NT)
            pool.dma_start(skT, A["keys"][0]).then_inc(keys_in, 16)
            peer_head(0)
            pool.wait_ge(x_updated, 12)
            pool.dma_start(ckT, A["cache_kT"]).then_inc(caches_in, 16)
            pool.dma_start(cv, A["cache_v"]).then_inc(caches_in, 16)
            pool.dma_start(ropec, A["rope"]).then_inc(caches_in, 16)
            pool.dma_start(lamv, A["diff_lam"].partition_broadcast(P)).then_inc(caches_in, 16)
            pool.wait_ge(krow_ready, 2)
            pool.dma_start(A["out_k"], krow).then_inc(outs_done, 16)
            pool.wait_ge(v_taken, 6)
            pool.dma_start(A["out_v"], vrow[:, 0, :]).then_inc(outs_done, 16)
            pool.wait_ge(outs_done, 64)
            pool.wait_ge(hT_by_dve, 4 * NT)
            pool.dma_start(skT, A["keys"][1]).then_inc(keys_in, 16)
            peer_head(1)
            pool.wait_ge(x_updated, 19)
            pool.dma_start(fin_g, A["final_norm"].partition_broadcast(P)).then_inc(fin_in, 16)
            pool.wait_ge(xn_ready, NT * 4 + 1)
            pool.dma_start(A["y_prompt"], xn[:, 0, :]).then_inc(outs_done, 16)
            pool.wait_ge(xn_ready, NT * 4 + 3)
            pool.dma_start(A["y_sample"].rearrange("(t p) d -> p t d", p=P), xn[:, 1:3, :]).then_inc(outs_done, 16)
            pool.wait_ge(outs_done, 96)


def kernel(**inputs):
    import numpy as np
    import concourse.bacc as bacc
    from concourse.bass_utils import run_bass_kernel_spmd

    z = {k: np.asarray(v) for k, v in inputs.items()}

    def cols(a):
        return np.asarray(a).reshape(-1, P).T

    def stationary(w):
        n = w.shape[1] // P
        return w.reshape(DC, P, n, P).transpose(2, 1, 0, 3).reshape(n, P, D)

    def moving(w):
        n = w.shape[1] // 512
        return w.reshape(4, 2, P, n, 512).transpose(3, 0, 2, 1, 4).reshape(4 * n, P, D)

    arr = {}
    cond = np.stack([z["c_ctx"], z["c"][0]])
    b_ada = z["b_ada"].reshape(2, 48, P).transpose(2, 0, 1).reshape(P, 96)
    feats = [cols(z["rwkv_w0"]), cols(z["rwkv_a0"]), cols(z["rwkv_k_k"]), cols(z["rwkv_k_a"]), cols(z["rwkv_r_k"]),
             cols(z["rwkv_ln_g"]), cols(z["rwkv_ln_b"]), cols(z["conv_w"]), cols(z["norm_mix"]), cols(z["norm_ffn"]),
             b_ada, cond.reshape(2, DC, P).transpose(2, 1, 0).reshape(P, 16), cols(z["diff_subln"]),
             np.tile(np.array([[NORM_EPS, GN_EPS]], np.float32), (P, 1))]
    arr["feats"] = np.concatenate(feats, axis=1)
    a = np.arange(P)
    up = (a[None, :] > a[:, None]).astype(np.float32)
    eye = np.eye(P, dtype=np.float32)
    rot = np.zeros((P, P), np.float32)
    q = HD // 4
    for base in (0, HD):
        for g in (0, 2 * q):
            for i in range(q):
                rot[base + g + q + i, base + g + i] = -1.0
                rot[base + g + i, base + g + q + i] = 1.0
    consts = {"ident": eye, "ones": np.ones((P, P), np.float32),
              "head_ones": (a[:, None] // HD == a[None, :] // HD).astype(np.float32),
              "iota": np.tile(a.astype(np.float32), (P, 1)), "rot": rot, "upper": up, "lower": up.T,
              "upper_eq": up + eye, "lower_eq": up.T + eye}
    arr["const"] = np.stack([consts[n] for n in CONST], axis=1)
    lev = np.zeros((P, 2, LEVELS, P), np.float32)
    for lv in range(LEVELS):
        b = 1 << lv
        off = ((a[:, None] // (2 * b) == a[None, :] // (2 * b)) & (a[:, None] // b > a[None, :] // b)).astype(np.float32)
        lev[:, 0, lv, :] = off
        lev[:, 1, lv, :] = off.T
    arr["levels"] = lev
    rowp, colp = np.repeat(np.arange(4, dtype=np.float32), 64), np.tile(np.arange(64, dtype=np.float32), 4)
    inv = (np.float32(10000.0) ** (-np.arange(16, dtype=np.float32) / np.float32(16))).astype(np.float32)
    ar, ac = rowp[:, None] * inv[None, :], colp[:, None] * inv[None, :]
    ang = np.concatenate([ar, ar, ac, ac], axis=-1)
    cs = np.stack([np.cos(ang), np.sin(ang)]).transpose(2, 0, 1)
    arr["rope"] = np.concatenate([cs, cs], axis=0).astype(np.float32)
    sm = np.ones((P, T), np.float32)
    sm[:, ::P] = 0.0
    arr["scan_mask"] = sm
    arr["lora"] = np.concatenate([z["rwkv_w_up"][0].transpose(1, 0, 2), z["rwkv_a_up"][0].transpose(1, 0, 2)], axis=0)
    arr["gup"] = z["rwkv_g_up"][0]
    arr["final_norm"] = z["final_norm"]
    arr["x_prompt"] = z["x_prompt"][0]
    arr["x_sample"] = z["x_sample"][0]
    arr["state"] = z["state_rwkv"][0, 0].reshape(2, NF, 2, HD, HD).transpose(2, 4, 0, 1, 3).reshape(P, 2, NF, HD)
    arr["cache_kT"] = z["cache_k"][0, 0].reshape(P, NH, P).transpose(2, 1, 0)
    arr["cache_v"] = z["cache_v"][0, 0].reshape(P, D)
    arr["diff_lam"] = z["diff_lam"][0].reshape(4 * HD)
    arr["keys"] = z["peer_sub_keys"].reshape(2, 16, P, P).transpose(0, 3, 1, 2)
    for layer in range(2):
        arr[f"ada{layer}"] = moving(z["w_ada"][layer])
        arr[f"query{layer}"] = stationary(z["peer_w_q"][layer])
        arr[f"mix_out{layer}"] = moving(z["w_out_even" if layer == 0 else "w_out_odd"][0])
        arr[f"u{layer}"] = z["peer_u"][layer].reshape(P, NJ, DC, P).transpose(1, 3, 2, 0).reshape(NJ, P, D)
        arr[f"v{layer}"] = z["peer_v"][layer].reshape(P, NJ, D).transpose(1, 0, 2)
    arr["mix_in0"] = stationary(z["w_in_even"][0])
    wo = z["w_in_odd"][0]
    arr["mix_in1"], arr["mix_v1"] = stationary(wo[:, 0:2 * D]), moving(wo[:, 2 * D:])
    arr = {k: np.ascontiguousarray(v) for k, v in arr.items()}

    nc = bacc.Bacc("TRN2", target_bir_lowering=False, num_devices=1)
    A = {}
    for k, v in arr.items():
        A[k] = nc.dram_tensor(f"in_{k}", v.shape, mybir.dt.from_np(v.dtype), kind="ExternalInput").ap()
    outs = {"y_prompt": (P, D), "y_sample": (2 * P, D), "out_state": (2, P, NF, HD), "out_k": (P, D), "out_v": (P, D)}
    for k, shape in outs.items():
        A[k] = nc.dram_tensor(k, shape, F32, kind="ExternalOutput").ap()
    build(nc, A)
    r = run_bass_kernel_spmd(nc, [{f"in_{k}": v for k, v in arr.items()}], core_ids=[0]).results[0]
    st = r["out_state"].reshape(2, 2, HD, NF, HD)
    st = st.transpose(0, 3, 1, 4, 2).reshape(1, 1, 2, NH, HD, HD)
    return (r["y_prompt"].reshape(1, P, D), r["y_sample"].reshape(1, 2 * P, D), np.ascontiguousarray(st),
            r["out_k"].reshape(1, 1, P, NH, 2, HD), r["out_v"].reshape(1, 1, P, NH, 2 * HD))
```
